# Optimizing a Trainium2 kernel written in Bass

```python
import jax, jax.numpy as jnp
from jax import lax
import numpy as np
import math

D_MODEL = 2048
BATCH = 1
SEQ = 256
DEPTH = 1

GRID_W = 64
MIX_WIDTH = D_MODEL
CONV_WIDTH = MIX_WIDTH // 2
NA_HEADS = 16
NA_HEAD_DIM = (MIX_WIDTH - CONV_WIDTH) // NA_HEADS
NA_WIDTH = NA_HEADS * NA_HEAD_DIM
CONV_KERNEL = 31
WIN_ROWS_MAX = 8
WIN_COLS = 16
D_FF = 4 * D_MODEL
IN_COLS = 2 * CONV_WIDTH + 3 * NA_WIDTH
RMS_EPS = 1e-6
LN_EPS = 1e-5
NEG_INF = -1e30


def rms_norm(x, g):
    xf = x.astype(jnp.float32)
    y = xf * lax.rsqrt(jnp.mean(xf * xf, axis=-1, keepdims=True) + RMS_EPS)
    return (y * g.astype(jnp.float32)).astype(x.dtype)

def layer_norm(x, g, b):
    xf = x.astype(jnp.float32)
    mu = jnp.mean(xf, axis=-1, keepdims=True)
    xc = xf - mu
    var = jnp.mean(xc * xc, axis=-1, keepdims=True)
    y = xc * lax.rsqrt(var + LN_EPS) * g.astype(jnp.float32) + b.astype(jnp.float32)
    return y.astype(x.dtype)

def conformer_conv_group(a, gate, w_dw, b_dw, ln_g, ln_b):
    u = a * jax.nn.sigmoid(gate)
    u = lax.conv_general_dilated(
        u, w_dw[:, None, :].astype(u.dtype),
        window_strides=(1,),
        padding=[(CONV_KERNEL // 2, CONV_KERNEL // 2)],
        dimension_numbers=("NWC", "WIO", "NWC"),
        feature_group_count=CONV_WIDTH,
    ) + b_dw.astype(u.dtype)
    return jax.nn.silu(layer_norm(u, ln_g, ln_b))

def neighbourhood_attention_group(q, k, v, rpb):
    B, T, _ = q.shape
    rows = T // GRID_W
    kr = min(WIN_ROWS_MAX, rows)
    r = np.arange(rows)
    c = np.arange(GRID_W)
    row_start = np.clip(r - kr // 2, 0, rows - kr)
    row_idx = row_start[:, None] + np.arange(kr)[None, :]
    col_start = np.clip(c - WIN_COLS // 2, 0, GRID_W - WIN_COLS)
    col_mask = (c[None, :] >= col_start[:, None]) & (c[None, :] < col_start[:, None] + WIN_COLS)
    dr = row_idx - r[:, None] + (WIN_ROWS_MAX - 1)
    dc = np.clip(c[None, :] - c[:, None], -(WIN_COLS - 1), WIN_COLS - 1) + (WIN_COLS - 1)
    bias = rpb[:, dr[:, None, :, None], dc[None, :, None, :]].astype(jnp.float32)

    def to_grid(t):
        return t.reshape(B, rows, GRID_W, NA_HEADS, NA_HEAD_DIM)

    qg, kg, vg = to_grid(q), to_grid(k), to_grid(v)
    k_rows = kg[:, row_idx]
    v_rows = vg[:, row_idx]
    s = jnp.einsum("brwhd,brkvhd->bhrwkv", qg, k_rows,
                   preferred_element_type=jnp.float32) * (NA_HEAD_DIM ** -0.5)
    s = jnp.where(col_mask[:, None, :], s + bias, NEG_INF)
    p = jax.nn.softmax(s.reshape(B, NA_HEADS, rows, GRID_W, kr * GRID_W), axis=-1)
    p = p.reshape(s.shape).astype(v.dtype)
    o = jnp.einsum("bhrwkv,brkvhd->brwhd", p, v_rows)
    return o.reshape(B, T, NA_WIDTH)

def first_inputs(seed: int = 0) -> dict:
    key = jax.random.key(seed)
    ks = jax.random.split(key, 16)
    f32 = jnp.float32
    x = jax.random.normal(ks[0], (BATCH, SEQ, D_MODEL), f32)
    w_in = jax.random.normal(ks[1], (DEPTH, D_MODEL, IN_COLS), f32) * D_MODEL ** -0.5
    w_dw = jax.random.normal(ks[2], (DEPTH, CONV_KERNEL, CONV_WIDTH), f32) * CONV_KERNEL ** -0.5
    b_dw = jax.random.normal(ks[3], (DEPTH, CONV_WIDTH), f32) * 0.01
    conv_ln_g = 1.0 + 0.05 * jax.random.normal(ks[4], (DEPTH, CONV_WIDTH), f32)
    conv_ln_b = 0.01 * jax.random.normal(ks[5], (DEPTH, CONV_WIDTH), f32)
    rpb = 0.02 * jax.random.normal(ks[6], (DEPTH, NA_HEADS, 2 * WIN_ROWS_MAX - 1, 2 * WIN_COLS - 1), f32)
    w_out = jax.random.normal(ks[7], (DEPTH, MIX_WIDTH, D_MODEL), f32) * MIX_WIDTH ** -0.5
    w_up = jax.random.normal(ks[8], (DEPTH, D_MODEL, D_FF), f32) * D_MODEL ** -0.5
    w_down = jax.random.normal(ks[9], (DEPTH, D_FF, D_MODEL), f32) * D_FF ** -0.5
    pre_mix_g = 1.0 + 0.05 * jax.random.normal(ks[10], (DEPTH, D_MODEL), f32)
    post_mix_g = 1.0 + 0.05 * jax.random.normal(ks[11], (DEPTH, D_MODEL), f32)
    pre_mlp_g = 1.0 + 0.05 * jax.random.normal(ks[12], (DEPTH, D_MODEL), f32)
    post_mlp_g = 1.0 + 0.05 * jax.random.normal(ks[13], (DEPTH, D_MODEL), f32)
    return {"x": x, "w_in": w_in, "w_dw": w_dw, "b_dw": b_dw, "conv_ln_g": conv_ln_g,
            "conv_ln_b": conv_ln_b, "rpb": rpb, "w_out": w_out, "w_up": w_up, "w_down": w_down,
            "pre_mix_g": pre_mix_g, "post_mix_g": post_mix_g, "pre_mlp_g": pre_mlp_g,
            "post_mlp_g": post_mlp_g}

def first_block(x, w_in, w_dw, b_dw, conv_ln_g, conv_ln_b, rpb, w_out, w_up, w_down,
              pre_mix_g, post_mix_g, pre_mlp_g, post_mlp_g):
    splits = [CONV_WIDTH, 2 * CONV_WIDTH, 2 * CONV_WIDTH + NA_WIDTH, 2 * CONV_WIDTH + 2 * NA_WIDTH]
    for l in range(DEPTH):
        h = rms_norm(x, pre_mix_g[l])
        proj = h @ w_in[l]
        a, gate, q, k, v = jnp.split(proj, splits, axis=-1)
        yc = conformer_conv_group(a, gate, w_dw[l], b_dw[l], conv_ln_g[l], conv_ln_b[l])
        ya = neighbourhood_attention_group(q, k, v, rpb[l])
        mix = jnp.concatenate([yc, ya], axis=-1) @ w_out[l]
        x = x + rms_norm(mix, post_mix_g[l])
        h = rms_norm(x, pre_mlp_g[l])
        f = jnp.square(jax.nn.relu(h @ w_up[l])) @ w_down[l]
        x = x + rms_norm(f, post_mlp_g[l])
    return x


H_A = 8
DQK_A = 128
DV_A = 256
D_A = H_A * DV_A
QK_A = H_A * DQK_A
CHUNK = 64
CONV_K = 4
H_B = 16
D_NOPE = 128
D_ROPE = 64
D_HQK = D_NOPE + D_ROPE
D_VB = 128
D_B = H_B * D_VB
Q_LORA = 512
KV_LORA = 512
Q_BLOCK = 128
ROPE_THETA = 10000.0
EPS = 1e-6
NEG_INF_2 = -1e30
SPLIT_SIZES = (QK_A, QK_A, D_A, D_A, H_A, H_A, D_A, Q_LORA, KV_LORA, D_ROPE, D_B, D_MODEL, D_MODEL)
N_IN = sum(SPLIT_SIZES)


def rms_norm_2(x, g):
    x32 = x.astype(jnp.float32)
    y = x32 * lax.rsqrt(jnp.mean(x32 * x32, axis=-1, keepdims=True) + EPS)
    return (y * g.astype(jnp.float32)).astype(x.dtype)

def causal_depthwise_conv(x, w):
    s_len = x.shape[1]
    xp = jnp.pad(x, ((0, 0), (CONV_K - 1, 0), (0, 0)))
    out = xp[:, CONV_K - 1:] * w[CONV_K - 1]
    for j in range(CONV_K - 1):
        out = out + xp[:, j:j + s_len] * w[j]
    return out

def rope_tables(positions):
    inv_freq = jnp.exp(-math.log(ROPE_THETA) * jnp.arange(0, D_ROPE, 2, dtype=jnp.float32) / D_ROPE)
    ang = positions.astype(jnp.float32)[..., None] * inv_freq
    return jnp.cos(ang)[:, :, None, :], jnp.sin(ang)[:, :, None, :]

def apply_rope(x, cos, sin):
    x32 = x.astype(jnp.float32)
    x1, x2 = jnp.split(x32, 2, axis=-1)
    return jnp.concatenate([x1 * cos - x2 * sin, x2 * cos + x1 * sin], axis=-1).astype(x.dtype)

def mlstm_chunkwise(q, k, v, i_pre, f_pre):
    b_sz, s_len, n_h, dk = q.shape
    dv = v.shape[-1]
    n_chunks = s_len // CHUNK
    f32 = jnp.float32

    def chunks(t):
        t = t.astype(f32).reshape((b_sz, n_chunks, CHUNK, n_h) + t.shape[3:])
        return jnp.moveaxis(t, (1, 3), (0, 2))

    qc_all = chunks(q) * (dk ** -0.5)
    kc_all = chunks(k)
    vc_all = chunks(v)
    ic_all = chunks(i_pre)
    lf_all = jax.nn.log_sigmoid(chunks(f_pre))
    causal = jnp.tril(jnp.ones((CHUNK, CHUNK), dtype=bool))

    def step(carry, xs):
        c_st, n_st, m_st = carry
        qc, kc, vc, ic, fc = xs
        b = jnp.cumsum(fc, axis=-1)
        g = b[..., -1]
        d = jnp.where(causal, b[..., :, None] - b[..., None, :] + ic[..., None, :], NEG_INF_2)
        inter = b + m_st[..., None]
        m_i = jnp.maximum(jnp.max(d, axis=-1), inter)
        s = jnp.einsum('bhid,bhjd->bhij', qc, kc) * jnp.exp(d - m_i[..., None])
        decay = jnp.exp(inter - m_i)
        num = jnp.einsum('bhij,bhje->bhie', s, vc) + decay[..., None] * jnp.einsum('bhid,bhde->bhie', qc, c_st)
        den = jnp.sum(s, axis=-1) + decay * jnp.einsum('bhid,bhd->bhi', qc, n_st)
        h = num / jnp.maximum(jnp.abs(den), jnp.exp(-m_i))[..., None]
        w = g[..., None] - b + ic
        m_new = jnp.maximum(g + m_st, jnp.max(w, axis=-1))
        carry_scale = jnp.exp(g + m_st - m_new)
        kw = kc * jnp.exp(w - m_new[..., None])[..., None]
        c_new = carry_scale[..., None, None] * c_st + jnp.einsum('bhjd,bhje->bhde', kw, vc)
        n_new = carry_scale[..., None] * n_st + jnp.sum(kw, axis=-2)
        return (c_new, n_new, m_new), h

    init = (jnp.zeros((b_sz, n_h, dk, dv), f32), jnp.zeros((b_sz, n_h, dk), f32), jnp.zeros((b_sz, n_h), f32))
    _, h_all = lax.scan(step, init, (qc_all, kc_all, vc_all, ic_all, lf_all))
    h_all = jnp.moveaxis(h_all, (0, 2), (1, 3)).reshape(b_sz, s_len, n_h, dv)
    return h_all.astype(v.dtype)

def causal_attention(q, k, v):
    b_sz, s_len, n_h, dq = q.shape
    n_blocks = s_len // Q_BLOCK
    scale = dq ** -0.5
    key_idx = jnp.arange(s_len)
    q_blocks = jnp.moveaxis(q.reshape(b_sz, n_blocks, Q_BLOCK, n_h, dq), 1, 0)

    def one_block(args):
        q_blk, blk_id = args
        q_idx = blk_id * Q_BLOCK + jnp.arange(Q_BLOCK)
        s = jnp.einsum('bqhd,bkhd->bhqk', q_blk, k).astype(jnp.float32) * scale
        s = jnp.where(key_idx[None, :] <= q_idx[:, None], s, NEG_INF_2)
        p = jax.nn.softmax(s, axis=-1).astype(v.dtype)
        return jnp.einsum('bhqk,bkhd->bqhd', p, v)

    o = lax.map(one_block, (q_blocks, jnp.arange(n_blocks)))
    return jnp.moveaxis(o, 0, 1).reshape(b_sz, s_len, n_h, v.shape[-1])

def hybrid_layer(x, cos, sin, norm_g, w_in, gate_bias, conv_w, mlstm_norm_g, w_a,
                 q_lat_g, kv_lat_g, w_uq, w_ukv, q_norm_g, k_norm_g, w_b, w_out):
    b_sz, s_len, _ = x.shape
    h = rms_norm_2(x, norm_g)
    proj = jnp.einsum('bsd,dn->bsn', h, w_in)
    offsets = [int(o) for o in np.cumsum(SPLIT_SIZES)[:-1]]
    (q_a, k_a, v_a, o_a, i_a, f_a, z_a, c_q, c_kv, k_r, z_b, g_a, g_b) = jnp.split(proj, offsets, axis=-1)

    qk_a = jax.nn.silu(causal_depthwise_conv(jnp.concatenate([q_a, k_a], axis=-1), conv_w))
    q_a, k_a = jnp.split(qk_a, 2, axis=-1)
    h_a = mlstm_chunkwise(q_a.reshape(b_sz, s_len, H_A, DQK_A),
                          k_a.reshape(b_sz, s_len, H_A, DQK_A),
                          v_a.reshape(b_sz, s_len, H_A, DV_A),
                          i_a + gate_bias[:H_A], f_a + gate_bias[H_A:])
    h_a = rms_norm_2(h_a, mlstm_norm_g.reshape(H_A, DV_A)).reshape(b_sz, s_len, D_A)
    y_a = jnp.einsum('bsc,cd->bsd', jax.nn.sigmoid(o_a) * h_a * jax.nn.silu(z_a), w_a)

    q_b = jnp.einsum('bsr,rn->bsn', rms_norm_2(c_q, q_lat_g), w_uq).reshape(b_sz, s_len, H_B, D_HQK)
    kv_b = jnp.einsum('bsr,rn->bsn', rms_norm_2(c_kv, kv_lat_g), w_ukv).reshape(b_sz, s_len, H_B, D_NOPE + D_VB)
    k_nope, v_b = jnp.split(kv_b, [D_NOPE], axis=-1)
    k_b = jnp.concatenate([k_nope, jnp.broadcast_to(k_r[:, :, None, :], (b_sz, s_len, H_B, D_ROPE))], axis=-1)
    q_b = rms_norm_2(q_b, q_norm_g)
    k_b = rms_norm_2(k_b, k_norm_g)
    q_b = jnp.concatenate([q_b[..., :D_NOPE], apply_rope(q_b[..., D_NOPE:], cos, sin)], axis=-1)
    k_b = jnp.concatenate([k_b[..., :D_NOPE], apply_rope(k_b[..., D_NOPE:], cos, sin)], axis=-1)
    o_b = causal_attention(q_b, k_b, v_b).reshape(b_sz, s_len, D_B)
    y_b = jnp.einsum('bsc,cd->bsd', o_b * jax.nn.silu(z_b), w_b)

    y = jax.nn.sigmoid(g_a) * y_a + jax.nn.sigmoid(g_b) * y_b
    return x + jnp.einsum('bsd,de->bse', y, w_out)

def second_inputs(seed: int = 0) -> dict:
    key = jax.random.key(seed)
    ks = jax.random.split(key, 16)
    f32 = jnp.float32

    def nrm(k, shape, scale):
        return jax.random.normal(k, shape, f32) * scale

    x = nrm(ks[0], (BATCH, SEQ, D_MODEL), 1.0)
    positions = (jax.random.randint(ks[1], (BATCH, 1), 0, 1024, dtype=jnp.int32)
                 + jnp.arange(SEQ, dtype=jnp.int32)[None, :])
    norm_g = 1.0 + nrm(ks[2], (DEPTH, D_MODEL), 0.02)
    w_in = nrm(ks[3], (DEPTH, D_MODEL, N_IN), D_MODEL ** -0.5)
    kb1, kb2 = jax.random.split(ks[4])
    gate_bias = jnp.concatenate([nrm(kb1, (DEPTH, H_A), 0.1),
                                 jnp.linspace(3.0, 6.0, H_A, dtype=f32)[None, :] + nrm(kb2, (DEPTH, H_A), 0.1)], axis=-1)
    conv_w = nrm(ks[5], (DEPTH, CONV_K, 2 * QK_A), CONV_K ** -0.5)
    mlstm_norm_g = 1.0 + nrm(ks[6], (DEPTH, D_A), 0.02)
    w_a = nrm(ks[7], (DEPTH, D_A, D_MODEL), D_A ** -0.5)
    q_lat_g = 1.0 + nrm(ks[8], (DEPTH, Q_LORA), 0.02)
    kv_lat_g = 1.0 + nrm(ks[9], (DEPTH, KV_LORA), 0.02)
    w_uq = nrm(ks[10], (DEPTH, Q_LORA, H_B * D_HQK), Q_LORA ** -0.5)
    w_ukv = nrm(ks[11], (DEPTH, KV_LORA, H_B * (D_NOPE + D_VB)), KV_LORA ** -0.5)
    q_norm_g = 1.0 + nrm(ks[12], (DEPTH, D_HQK), 0.02)
    k_norm_g = 1.0 + nrm(ks[13], (DEPTH, D_HQK), 0.02)
    w_b = nrm(ks[14], (DEPTH, D_B, D_MODEL), D_B ** -0.5)
    w_out = nrm(ks[15], (DEPTH, D_MODEL, D_MODEL), D_MODEL ** -0.5)
    return {"x": x, "positions": positions, "norm_g": norm_g, "w_in": w_in, "gate_bias": gate_bias,
            "conv_w": conv_w, "mlstm_norm_g": mlstm_norm_g, "w_a": w_a, "q_lat_g": q_lat_g,
            "kv_lat_g": kv_lat_g, "w_uq": w_uq, "w_ukv": w_ukv, "q_norm_g": q_norm_g,
            "k_norm_g": k_norm_g, "w_b": w_b, "w_out": w_out}

def second_block(x, positions, norm_g, w_in, gate_bias, conv_w, mlstm_norm_g, w_a, q_lat_g,
              kv_lat_g, w_uq, w_ukv, q_norm_g, k_norm_g, w_b, w_out):
    cos, sin = rope_tables(positions)
    for l in range(DEPTH):
        x = hybrid_layer(x, cos, sin, norm_g[l], w_in[l], gate_bias[l], conv_w[l], mlstm_norm_g[l],
                         w_a[l], q_lat_g[l], kv_lat_g[l], w_uq[l], w_ukv[l], q_norm_g[l],
                         k_norm_g[l], w_b[l], w_out[l])
    return x


def setup_inputs(seed=0):
    out = dict(first_inputs(seed))
    for name, value in second_inputs(seed + 1).items():
        if name != "x":
            out[name + "_2"] = value
    return out


def reference(
    x, w_in, w_dw, b_dw, conv_ln_g, conv_ln_b, rpb, w_out, w_up, w_down, pre_mix_g, post_mix_g,
    pre_mlp_g, post_mlp_g, positions_2, norm_g_2, w_in_2, gate_bias_2, conv_w_2, mlstm_norm_g_2,
    w_a_2, q_lat_g_2, kv_lat_g_2, w_uq_2, w_ukv_2, q_norm_g_2, k_norm_g_2, w_b_2, w_out_2,
):
    x = first_block(
        x, w_in, w_dw, b_dw, conv_ln_g, conv_ln_b, rpb, w_out, w_up, w_down, pre_mix_g,
        post_mix_g, pre_mlp_g, post_mlp_g,
    )
    return second_block(
        x, positions_2, norm_g_2, w_in_2, gate_bias_2, conv_w_2, mlstm_norm_g_2, w_a_2,
        q_lat_g_2, kv_lat_g_2, w_uq_2, w_ukv_2, q_norm_g_2, k_norm_g_2, w_b_2, w_out_2,
    )


_drawn_inputs = setup_inputs


def setup_inputs(seed=0):
    import zlib

    import numpy as np

    out = dict(_drawn_inputs(seed))
    spreads = {}
    factors = {'b_dw': 4.26,
     'conv_ln_b': 7.153,
     'rpb': 8.0,
     'norm_g_2': 8.0,
     'mlstm_norm_g_2': 8.0,
     'q_lat_g_2': 8.0,
     'kv_lat_g_2': 8.0,
     'q_norm_g_2': 8.0,
     'k_norm_g_2': 8.0}
    for name, (base, spread) in spreads.items():
        noise = np.random.default_rng([zlib.crc32(name.encode()), seed]).standard_normal(out[name].shape)
        drawn = base * np.exp(spread * noise) if base else spread * noise
        out[name] = __import__('jax').numpy.asarray(drawn.astype(out[name].dtype))
    for name, factor in factors.items():
        out[name] = (out[name] * factor).astype(out[name].dtype)
    return out
```

```python
from contextlib import ExitStack

import numpy as np

import concourse.bass as bass
from concourse import mybir

F32 = mybir.dt.float32
F32R = mybir.dt.float32r
I32 = mybir.dt.int32
ALU = mybir.AluOpType
ACT = mybir.ActivationFunctionType
AX = mybir.AxisListType

P = 128
NB = 512
NEG = -1e30
RAW = 5
RING = 5
AHEAD = RING - 1
SBANKS = 4

VEC = {}
_at = 0
for _name, _n in (("pre_mix_g", 16), ("pre_mlp_g", 16), ("norm_g_2", 16), ("mlstm_g", 16), ("ln_g", 8), ("ln_b", 8),
                  ("b_dw", 8), ("w_dw", 248), ("conv_w", 64), ("q_lat_g", 4), ("kv_lat_g", 4), ("gqn", 1), ("gkn", 1),
                  ("gqr", 64), ("gkr", 64), ("gb", 2)):
    VEC[_name] = (_at, _at + _n)
    _at += _n
NVEC = _at
C_ID, C_MASK, C_MASKT, C_INVF = 0, 128, 512, 640
NCST = 672


class Tok:

    def __init__(self):
        self.sem, self.val, self.used = None, None, False


class Queue:

    def __init__(self, sem):
        self.sem, self.ops = sem, []

    def __call__(self, fn, *waits):
        flat = []
        stack = list(waits)
        while stack:
            w = stack.pop()
            if w is None:
                continue
            if isinstance(w, (list, tuple)):
                stack.extend(w)
            else:
                flat.append(w)
                w.used = True
        t = Tok()
        self.ops.append((fn, flat, t))
        return t

    def count(self):
        n = 0
        for _, _, t in self.ops:
            if t.used and t.sem is None:
                n += 1
                t.sem, t.val = self.sem, n

    def write(self, eng):
        seen = {}
        for fn, waits, t in self.ops:
            need = {}
            for w in waits:
                if need.get(id(w.sem), (None, 0))[1] < w.val:
                    need[id(w.sem)] = (w.sem, w.val)
            for k, (s, v) in need.items():
                if seen.get(k, 0) < v:
                    eng.wait_ge(s, v)
                    seen[k] = v
            ins = fn(eng)
            if t.used and t.sem is self.sem:
                ins.then_inc(self.sem, 1)


class Slots:

    def __init__(self, bufs):
        self.bufs, self.after, self.out, self.at = bufs, [[] for _ in bufs], [False] * len(bufs), 0

    def avail(self, n=1):
        return all(not self.out[(self.at + i) % len(self.bufs)] for i in range(n))

    def get(self):
        i = self.at % len(self.bufs)
        assert not self.out[i]
        self.out[i] = True
        self.at += 1
        return i, self.bufs[i], self.after[i]

    def give(self, i, *tokens):
        self.after[i] = list(tokens)
        self.out[i] = False


class TBuf:

    def __init__(self, hi, lo):
        self.hi, self.lo = hi, lo
        self.ready = [None] * 16
        self.read = [[] for _ in range(16)]


def bass_two_blocks(nc, d, out, dbg=None):
    ctx = ExitStack()
    with ctx:
        def sb(name, shape, dt=F32):
            return ctx.enter_context(nc.sbuf_tensor(name, shape, dt))

        def sem(name):
            return ctx.enter_context(nc.semaphore(name))

        raw = [sb(f"raw{i}", [P, 1024]) for i in range(RAW)]
        whi = [sb(f"whi{i}", [P, 1024], F32R) for i in range(RING)]
        wlo = [sb(f"wlo{i}", [P, 1024], F32R) for i in range(RING)]
        TA = TBuf(sb("ta_hi", [P, 16, 256], F32R), sb("ta_lo", [P, 16, 256], F32R))
        TB = TBuf(sb("tb_hi", [P, 16, 256], F32R), sb("tb_lo", [P, 16, 256], F32R))
        AR = sb("arena", [P, 17920])
        STAT = sb("stat", [P, 860])
        PS = sb("ps", [P, 720])
        CST = sb("cst", [P, NCST])
        VC = sb("vc", [P, NVEC])
        POS = sb("pos", [P, 2], I32)
        gps = [[ctx.enter_context(nc.psum_tensor(f"g{p}{t}", [P, NB], F32)) for t in range(2)] for p in range(2)]
        sps = [ctx.enter_context(nc.psum_tensor(f"s{i}", [P, NB], F32)) for i in range(SBANKS)]

        pe, act, dve, pool, sp = (Queue(sem(n)) for n in ("s_pe", "s_act", "s_dve", "s_pool", "s_sp"))
        counts = {}

        def dma(q, o, i, s, *waits):
            counts[s.name] = counts.get(s.name, 0) + 16
            q(lambda e: e.dma_start(o, i).then_inc(s, 16), *waits)
            t = Tok()
            t.sem, t.val = s, counts[s.name]
            return t

        def once(name, q, o, i, *waits):
            return dma(q, o, i, sem(name), *waits)

        def ar(a, n):
            return AR[:, a:a + n]

        def vec(name, i=0, n=1, parts=P):
            a = VEC[name][0] + i
            return VC[0:parts, a:a + n]

        ident = CST[:, C_ID:C_ID + P]
        nstat = [0]

        def stat(n):
            a = nstat[0]
            nstat[0] += n
            assert nstat[0] <= 860, nstat[0]
            return STAT[:, a:a + n]

        banks = Slots(sps)
        stage = Slots([ar(1024 * i, 1024) for i in range(4)])
        side = []

        def advance():
            for g in list(side):
                try:
                    next(g)
                except StopIteration:
                    side.remove(g)

        def spawn(g):
            next(g)
            side.append(g)

        def until(cond, what=""):
            n = 0
            while not cond():
                advance()
                n += 1
                assert n < 3000, what

        def drain():
            until(lambda: not side, "drain")

        def nat(buf, n=512):
            return buf.rearrange("p (t n) -> p t n", t=2) if n == 512 else buf

        t_cst = once("d_cst", act, CST[:, :], d["cst"])
        t_vec = once("d_vec", act, VC[:, :], d["vec"])
        t_pos = once("d_pos", act, POS[:, :], d["pos"])
        half = PS[:, 0:64]
        t_half = pool(lambda e: e.memset(half, -0.5))
        zero1 = PS[:, 64:65]
        t_z1 = pool(lambda e: e.memset(zero1, 0.0))

        units = []

        class Stripe:
            def __init__(self, name, w, n, kts, T, t0, evac, cols=NB, per=2, kfirst=0):
                self.name, self.evac, self.T, self.cols = name, evac, T, cols
                self.units = []
                for u in range(kts // per):
                    self.units.append(dict(st=self, src=d[w][n, kfirst + u] if w != "w_small" else d[w][u],
                                           kts=[t0 + u * per + k for k in range(per)], first=u == 0,
                                           last=u == kts // per - 1, size=per * cols))
                units.extend(self.units)

        raw_sem = [sem(f"d_raw{i}") for i in range(RAW)]
        raw_tok, hi_tok, lo_tok, mm_tok = {}, {}, {}, {}

        def issue_dma(u):
            if u >= len(units):
                return
            n = units[u]["size"]
            raw_tok[u] = dma(sp, raw[u % RAW][:, 0:n], units[u]["src"], raw_sem[u % RAW],
                             [hi_tok[u - RAW], lo_tok[u - RAW]] if u >= RAW else None)

        def issue_split(u):
            if u >= len(units):
                return
            n = units[u]["size"]
            r, h, l = raw[u % RAW][:, 0:n], whi[u % RING][:, 0:n], wlo[u % RING][:, 0:n]
            hi_tok[u] = act(lambda e: e.activation(h, r, ACT.Copy), raw_tok[u],
                            mm_tok[u - RING] if u >= RING else None)
            lo_tok[u] = dve(lambda e: e.tensor_tensor(l, r, h.bitcast(F32), ALU.subtract), hi_tok[u],
                            mm_tok[u - RING] if u >= RING else None)

        gfree = [[], []]
        nstripe = [0]

        def issue_mm(u):
            un = units[u]
            st, T, c = un["st"], un["st"].T, un["st"].cols
            if un["first"]:
                st.pair = nstripe[0] % 2
                nstripe[0] += 1
                until(lambda: gfree[st.pair] is not None, st.name + " psum")
                st.free, gfree[st.pair] = gfree[st.pair], None
            for kt in un["kts"]:
                until(lambda: T.ready[kt] is not None, f"{st.name} kt {kt}")
            first_wait = [hi_tok[u], lo_tok[u], st.free if un["first"] else None]
            for j, kt in enumerate(un["kts"]):
                wh = whi[u % RING][:, j * c:(j + 1) * c]
                wl = wlo[u % RING][:, j * c:(j + 1) * c]
                for t in range(2):
                    o = gps[st.pair][t][:, 0:c]
                    xh, xl = T.hi[:, kt, t * P:(t + 1) * P], T.lo[:, kt, t * P:(t + 1) * P]
                    a = un["first"] and j == 0
                    z = un["last"] and j == len(un["kts"]) - 1
                    pe(lambda e, o=o, x=xh, w=wh, a=a: e.matmul(o, x, w, start=a, stop=False),
                       first_wait, T.ready[kt])
                    first_wait = None
                    pe(lambda e, o=o, x=xh, w=wl: e.matmul(o, x, w, start=False, stop=False))
                    tok = pe(lambda e, o=o, x=xl, w=wh, z=z: e.matmul(o, x, w, start=False, stop=z))
                T.read[kt] = [tok]
            mm_tok[u] = tok
            if un["last"]:
                st.done = tok
                side.append(st.evac(st))

        def release(st, *tokens):
            gfree[st.pair] = list(tokens)

        def rsqrt_of(ss, n, eps, scale, w, *waits):
            v, r = stat(w), stat(w)
            a = dve(lambda e: e.tensor_scalar(v, ss, scale, eps, ALU.mult, ALU.add), *waits)
            b = pool(lambda e: e.tensor_tensor(r, v, half[:, 0:w], ALU.pow), a, t_half)
            return r, b

        def turn(src, srcw, T, kt0, g=None, scale=None, free=None):
            reads = []
            for pair in range(2):
                while not banks.avail():
                    yield
                i, b, after = banks.get()
                for k in range(2):
                    for t in range(2):
                        c = (2 * pair + k) * P
                        tok = pe(lambda e, o=b[:, k * 256 + t * P:k * 256 + (t + 1) * P], s=src[:, t, c:c + P]:
                                 e.transpose(o, s, ident), srcw, after, t_cst)
                reads.append(tok)
                if pair == 1 and free is not None:
                    free(reads)
                yield
                kt = kt0 + 2 * pair
                war = [T.read[kt], T.read[kt + 1]]
                if g is None:
                    h, l = T.hi[:, kt:kt + 2, :], T.lo[:, kt:kt + 2, :]
                    s = b[:, :].rearrange("p (k n) -> p k n", k=2)
                    if scale is None:
                        a = act(lambda e, h=h, s=s: e.activation(h, s, ACT.Copy), tok, war)
                        v = dve(lambda e, h=h, l=l, s=s: e.tensor_tensor(l, s, h.bitcast(F32), ALU.subtract), a, war)
                    else:
                        a = act(lambda e, h=h, s=s: e.activation(h, s, ACT.Copy, scale=scale), tok, war)
                        v = dve(lambda e, h=h, l=l, s=s: e.scalar_tensor_tensor(l, s, scale, h.bitcast(F32), ALU.mult,
                                                                                ALU.subtract), a, war)
                    T.ready[kt] = T.ready[kt + 1] = [a, v]
                    banks.give(i, a, v)
                else:
                    al = []
                    for k in range(2):
                        h, s = T.hi[:, kt + k, :], b[:, k * 256:(k + 1) * 256]
                        gg = vec(g[0], g[1] + 2 * pair + k)
                        a = act(lambda e, h=h, s=s, gg=gg: e.activation(h, s, ACT.Copy, scale=gg), tok, war, t_vec)
                    for k in range(2):
                        h, l, s = T.hi[:, kt + k, :], T.lo[:, kt + k, :], b[:, k * 256:(k + 1) * 256]
                        gg = vec(g[0], g[1] + 2 * pair + k)
                        v = dve(lambda e, h=h, l=l, s=s, gg=gg: e.scalar_tensor_tensor(
                            l, s, gg, h.bitcast(F32), ALU.mult, ALU.subtract), a, war, t_vec)
                        T.ready[kt + k] = [a, v]
                        al += [a, v]
                    banks.give(i, *al)

        def clear(T, a=0, b=16):
            for k in range(a, b):
                T.ready[k] = None

        def copy_scaled(st, dst, r, rw, waits):
            return [act(lambda e, t=t: e.activation(dst[:, t], gps[st.pair][t][:, 0:dst.shape[2]], ACT.Copy,
                                                    scale=r[:, t:t + 1]), st.done, rw, waits) for t in range(2)]

        def tanh_scaled(st, dst, r, rw, waits):
            return [act(lambda e, t=t: e.activation(dst[:, t], gps[st.pair][t][:, :], ACT.Tanh,
                                                    scale=r[:, t:t + 1]), st.done, rw, waits) for t in range(2)]

        def stage_get():
            i, b, after = stage.get()
            return i, nat(b), after

        def sumsq(src, waits, w):
            toks = []
            for t in range(2):
                toks.append(act(lambda e, t=t: e.activation(junk[:, 0:src.shape[2]], src[:, t], ACT.Square,
                                                            accum_out=w[:, t:t + 1]), waits, junk_tok[0]))
                junk_tok[0] = toks[-1]
            return toks

        junk = sb("junk", [P, 512])
        junk_tok = [None]

        def halved(r, rw):
            h = stat(2)
            return h, dve(lambda e: e.tensor_scalar(h, r, 0.5, None, ALU.mult), rw)

        S = {}
        X0 = ar(4096, 4096).rearrange("p (t n) -> p t n", t=2)
        QT1 = ar(4096, 2048).rearrange("p (c n) -> p c n", c=8)
        KT1 = ar(6144, 2048).rearrange("p (c n) -> p c n", c=8)
        V1 = ar(8192, 2048).rearrange("p (t n) -> p t n", t=2)
        UT = ar(10240, 2288).rearrange("p (c n) -> p c n", c=8)
        CV = ar(12528, 2048).rearrange("p (c n) -> p c n", c=8)
        LNN = ar(10240, 2048).rearrange("p (t n) -> p t n", t=2)
        na_bias = Slots([ar(14576 + 512 * i, 512) for i in range(2)])
        na_p = Slots([ar(15600 + 512 * i, 512) for i in range(2)])
        na_pt = Slots([ar(16624 + 512 * i, 512) for i in range(2)])
        na_bias_sem = [sem(f"d_bias{i}") for i in range(2)]
        xd = d["x"].rearrange("(t p) n -> p t n", p=P)

        def start1():
            ss4 = stat(8)
            ld = [once(f"d_x{c}", act, X0[:, :, c * 512:(c + 1) * 512], xd[:, :, c * 512:(c + 1) * 512])
                  for c in range(4)]
            S["x0_reads"] = []
            sq = []
            for c in range(4):
                g = turn(X0[:, :, c * 512:(c + 1) * 512], ld[c], TA, 4 * c, ("pre_mix_g", 4 * c),
                         free=S["x0_reads"].extend)
                sq += sumsq(X0[:, :, c * 512:(c + 1) * 512], ld[c], ss4[:, 2 * c:2 * c + 2])
                yield from g
            S["x0_reads"] += sq
            ss = stat(2)
            a = dve(lambda e: e.tensor_reduce(ss, ss4.rearrange("p (c t) -> p t c", t=2), AX.X, ALU.add), sq)
            r, rw = rsqrt_of(ss, 2, 1e-6, 1.0 / 2048, 2, a)
            S["r0"], S["r0w"] = r, rw
            S["r0h"], S["r0hw"] = halved(r, rw)

        gate_buf = {}
        t_upad = [dve(lambda e: e.memset(UT[:, :, 0:15], 0.0)), dve(lambda e: e.memset(UT[:, :, 271:286], 0.0))]
        conv_ready = [None] * 8

        def ev_gate(n):
            def f(st):
                while not stage.avail():
                    yield
                i, b, after = stage_get()
                t = tanh_scaled(st, b, S["r0h"], S["r0hw"], after)
                release(st, *t)
                gate_buf[n] = (i, b, t)
            return f

        def ev_a(n):
            def f(st):
                while not stage.avail():
                    yield
                i, b, after = stage_get()
                c = copy_scaled(st, b, S["r0h"], S["r0hw"], after)
                release(st, *c)
                gi, gb, gt = gate_buf.pop(n)
                u = dve(lambda e: e.scalar_tensor_tensor(b, gb, 1.0, b, ALU.add, ALU.mult), c, gt)
                stage.give(gi, u)
                yield
                for pair in range(2):
                    while not banks.avail():
                        yield
                    j, bk, baft = banks.get()
                    for k in range(2):
                        for t in range(2):
                            cc = (2 * pair + k) * P
                            tok = pe(lambda e, o=bk[:, k * 256 + t * P:k * 256 + (t + 1) * P], s=b[:, t, cc:cc + P]:
                                     e.transpose(o, s, ident), u, baft, t_cst)
                    yield
                    ct = 4 * n + 2 * pair
                    tk = act(lambda e, ct=ct, bk=bk: e.activation(
                        UT[:, ct:ct + 2, 15:271], bk[:, :].rearrange("p (k n) -> p k n", k=2), ACT.Copy), tok)
                    banks.give(j, tk)
                    conv_ready[ct] = conv_ready[ct + 1] = tk
                stage.give(i, tok)
                side.append(conv(n))
            return f

        conv_done = [None] * 8

        def conv(n):
            cts = range(4 * n, 4 * n + 4)
            last = {}
            for j in range(31):
                for ct in cts:
                    w = vec("w_dw", ct * 31 + j)
                    src, dst = UT[:, ct, j:j + 256], CV[:, ct, :]
                    if j == 0:
                        last[ct] = dve(lambda e, w=w, s=src, o=dst, ct=ct: e.tensor_scalar(
                            o, s, w, vec("b_dw", ct), ALU.mult, ALU.add), conv_ready[ct], t_vec, t_upad)
                    else:
                        last[ct] = dve(lambda e, w=w, s=src, o=dst: e.scalar_tensor_tensor(
                            o, s, w, o, ALU.mult, ALU.add), last[ct])
                yield
            for ct in cts:
                conv_done[ct] = last[ct]
            if n == 1:
                side.append(conv_ln())

        def conv_ln():
            while any(c is None for c in conv_done):
                yield
            st6 = [stat(12), stat(12)]
            mv = [stat(2), stat(2)]
            var = stat(2)
            cp, bn = [[], []], [[], []]
            for t in range(2):
                for hf in range(2):
                    while not banks.avail():
                        yield
                    j, bk, baft = banks.get()
                    for k in range(4):
                        tok = pe(lambda e, o=bk[:, k * P:(k + 1) * P], s=CV[:, 4 * hf + k, t * P:(t + 1) * P]:
                                 e.transpose(o, s, ident), conv_done, baft, t_cst)
                    yield
                    a = act(lambda e, t=t, hf=hf, bk=bk: e.activation(
                        LNN[:, t, hf * 512:(hf + 1) * 512], bk[:, :], ACT.Copy), tok, conv_done)
                    v = dve(lambda e, t=t, hf=hf, bk=bk: e.bn_stats(st6[t][:, 6 * hf:6 * hf + 6], bk[:, :]), a)
                    banks.give(j, a, v)
                    cp[t].append(a)
                    bn[t].append(v)
            ag = [dve(lambda e, t=t: e.bn_aggr(mv[t], st6[t].rearrange("p (a b) -> p a b", a=2)), bn[t])
                  for t in range(2)]
            yield
            vv = [dve(lambda e, t=t: e.tensor_scalar(var[:, t:t + 1], mv[t][:, 1:2], 1e-5, None, ALU.add), ag[t])
                  for t in range(2)]
            rs = stat(2)
            pw = pool(lambda e: e.tensor_tensor(rs, var, half[:, 0:2], ALU.pow), vv, t_half)
            yield
            nm = [dve(lambda e, t=t: e.tensor_scalar(LNN[:, t], LNN[:, t], mv[t][:, 0:1], rs[:, t:t + 1],
                                                     ALU.subtract, ALU.mult), pw, cp[t]) for t in range(2)]
            yield
            for pair in range(4):
                while not (banks.avail() and stage.avail()):
                    yield
                j, bk, baft = banks.get()
                i, zb, zaft = stage.get()
                for k in range(2):
                    for t in range(2):
                        cc = (2 * pair + k) * P
                        tok = pe(lambda e, o=bk[:, k * 256 + t * P:k * 256 + (t + 1) * P], s=LNN[:, t, cc:cc + P]:
                                 e.transpose(o, s, ident), nm, baft, t_cst)
                yield
                z, th = zb[:, 0:512], zb[:, 512:1024]
                za = [act(lambda e, k=k, bk=bk, z=z, ct=2 * pair + k: e.activation(
                    z[:, k * 256:(k + 1) * 256], bk[:, k * 256:(k + 1) * 256], ACT.Identity,
                    scale=vec("ln_g", ct), bias=vec("ln_b", ct)), tok, zaft, t_vec) for k in range(2)]
                banks.give(j, *za)
                ta = act(lambda e, z=z, th=th: e.activation(th, z, ACT.Tanh, scale=0.5), za)
                y = dve(lambda e, z=z, th=th: e.scalar_tensor_tensor(z, th, 1.0, z, ALU.add, ALU.mult), ta)
                yield
                kt = 2 * pair
                war = [TB.read[kt], TB.read[kt + 1]]
                h, l = TB.hi[:, kt:kt + 2, :], TB.lo[:, kt:kt + 2, :]
                s = z.rearrange("p (k n) -> p k n", k=2)
                a = act(lambda e, h=h, s=s: e.activation(h, s, ACT.Copy, scale=0.5), y, war)
                v = dve(lambda e, h=h, l=l, s=s: e.scalar_tensor_tensor(l, s, 0.5, h.bitcast(F32), ALU.mult,
                                                                        ALU.subtract), a, war)
                TB.ready[kt] = TB.ready[kt + 1] = [a, v]
                stage.give(i, a, v)

        qk_ready = {}

        def ev_qk(dst, key, n):
            def f(st):
                while not stage.avail():
                    yield
                i, b, after = stage_get()
                c = copy_scaled(st, b, S["r0"], S["r0w"], after)
                release(st, *c)
                yield
                for pair in range(2):
                    while not banks.avail():
                        yield
                    j, bk, baft = banks.get()
                    for k in range(2):
                        for t in range(2):
                            cc = (2 * pair + k) * P
                            tok = pe(lambda e, o=bk[:, k * 256 + t * P:k * 256 + (t + 1) * P], s=b[:, t, cc:cc + P]:
                                     e.transpose(o, s, ident), c, baft, t_cst)
                    yield
                    ct = 4 * n + 2 * pair
                    tk = act(lambda e, ct=ct, bk=bk: e.activation(
                        dst[:, ct:ct + 2, :], bk[:, :].rearrange("p (k n) -> p k n", k=2), ACT.Copy),
                        tok, S["x0_reads"])
                    banks.give(j, tk)
                    qk_ready[key, ct] = qk_ready[key, ct + 1] = tk
                stage.give(i, tok)
            return f

        v_ready = {}

        def ev_v(n):
            def f(st):
                c = copy_scaled(st, V1[:, :, n * 512:(n + 1) * 512], S["r0"], S["r0w"], None)
                release(st, *c)
                v_ready[n] = c
                side.append(na_heads(n))
                return
                yield
            return f

        na_out = {}

        def na_heads(n):
            while not stage.avail():
                yield
            i, b, after = stage_get()
            left = [8]
            outs = []
            for hh in range(8):
                while not (na_bias.avail() and na_p.avail() and na_pt.avail()):
                    yield
                spawn(na_head(8 * n + hh, b, after, outs, left))
                yield
            while left[0]:
                yield
            yield
            yield from turn(b, outs, TB, 8 + 4 * n, free=lambda r: stage.give(i, *r))

        na_last = []

        def na_head(h, ob, oaft, outs, left):
            ct, p0 = h // 2, 64 * (h % 2)
            bi, bb, baft = na_bias.get()
            pi, pb, paft = na_p.get()
            ti, tb, taft = na_pt.get()
            bl = dma(sp, bb, d["bias"][h], na_bias_sem[bi], baft)
            while (("q", ct) not in qk_ready) or (("k", ct) not in qk_ready) or not banks.avail():
                yield
            j, bk, kaft = banks.get()
            for it in range(2):
                tok = pe(lambda e, it=it: e.matmul(bk[:, it * 256:(it + 1) * 256],
                                                   QT1[p0:p0 + 64, ct, it * P:(it + 1) * P],
                                                   KT1[p0:p0 + 64, ct, :], start=True, stop=True),
                         qk_ready["q", ct], qk_ready["k", ct], kaft)
            na_last.append(tok)
            yield
            mx, sm, rc = stat(2), stat(2), stat(2)
            s = dve(lambda e: e.scalar_tensor_tensor(pb, bk[:, :], 0.125, bb, ALU.mult, ALU.add), tok, bl, paft)
            banks.give(j, s)
            na_bias.give(bi, s)
            p3 = pb.rearrange("p (t n) -> p t n", t=2)
            m = dve(lambda e: e.tensor_reduce(mx, p3, AX.X, ALU.max, negate=True), s)
            ex = [act(lambda e, t=t: e.activation(p3[:, t], p3[:, t], ACT.Exp, bias=mx[:, t:t + 1],
                                                  accum_out=sm[:, t:t + 1]), m) for t in range(2)]
            rr = dve(lambda e: e.reciprocal(rc, sm), ex)
            yield
            while not banks.avail():
                yield
            j, bk2, kaft = banks.get()
            for it in range(2):
                for jt in range(2):
                    tok = pe(lambda e, it=it, jt=jt: e.transpose(
                        bk2[:, jt * 256 + it * P:jt * 256 + (it + 1) * P], p3[:, it, jt * P:(jt + 1) * P], ident),
                        ex, kaft, t_cst)
            na_p.give(pi, tok)
            yield
            cp = act(lambda e: e.activation(tb, bk2[:, :], ACT.Copy), tok, taft)
            banks.give(j, cp)
            yield
            while not banks.avail():
                yield
            j, bk3, kaft = banks.get()
            for it in range(2):
                for jt in range(2):
                    tok = pe(lambda e, it=it, jt=jt: e.matmul(
                        bk3[:, it * 64:(it + 1) * 64], tb[:, jt * 256 + it * P:jt * 256 + (it + 1) * P],
                        V1[:, jt, h * 64:(h + 1) * 64], start=jt == 0, stop=jt == 1), cp, v_ready[h // 8], kaft)
            na_pt.give(ti, tok)
            na_last.append(tok)
            yield
            o = [act(lambda e, t=t: e.activation(ob[:, t, (h % 8) * 64:(h % 8 + 1) * 64],
                                                 bk3[:, t * 64:(t + 1) * 64], ACT.Copy, scale=rc[:, t:t + 1]),
                     tok, rr, oaft) for t in range(2)]
            banks.give(j, *o)
            outs.extend(o)
            left[0] -= 1

        FN = ar(4096, 4096).rearrange("p (t n) -> p t n", t=2)
        XR = ar(8192, 4096).rearrange("p (t n) -> p t n", t=2)
        PG = ar(12288, 2048)

        def norm_add(key, fg, sq, ss4, xw, gname, after_x):
            ss = stat(2)
            a = dve(lambda e: e.tensor_reduce(ss, ss4.rearrange("p (c t) -> p t c", t=2), AX.X, ALU.add), sq)
            r, rw = rsqrt_of(ss, 2, 1e-6, 1.0 / 2048, 2, a)
            xs4 = stat(8)
            xsq, reads = [], []
            for c in range(4):
                sl = slice(c * 512, (c + 1) * 512)
                ad = [dve(lambda e, t=t, sl=sl: e.scalar_tensor_tensor(
                    XR[:, t, sl], FN[:, t, sl], r[:, t:t + 1], XR[:, t, sl], ALU.mult, ALU.add), rw, fg[c], xw)
                    for t in range(2)]
                xsq += sumsq(XR[:, :, sl], ad, xs4[:, 2 * c:2 * c + 2])
                if after_x is not None:
                    reads.append(after_x(c, XR[:, :, sl], ad))
                yield from turn(XR[:, :, sl], ad, TA, 4 * c, (gname, 4 * c), free=reads.extend)
            S[key + "_x"] = ad
            S[key + "_reads"] = reads + xsq
            sx = stat(2)
            a = dve(lambda e: e.tensor_reduce(sx, xs4.rearrange("p (c t) -> p t c", t=2), AX.X, ALU.add), xsq)
            rx, rxw = rsqrt_of(sx, 2, 1e-6, 1.0 / 2048, 2, a)
            S[key], S[key + "w"] = rx, rxw
            S[key + "h"], S[key + "hw"] = halved(rx, rxw)

        mix_fg, mix_sq = [None] * 4, []
        mix_ss = stat(8)

        def ev_mix(n):
            def f(st):
                sl = slice(n * 512, (n + 1) * 512)
                w8 = mix_ss[:, 2 * n:2 * n + 2]
                if n == 0:
                    S["xr"] = once("d_xr", sp, XR, xd, na_last, TB.ready[0:8])
                    S["pg"] = once("d_pg", sp, PG, d["post_mix_g"], TB.ready[0:8], conv_done)
                for t in range(2):
                    k = act(lambda e, t=t: e.activation(junk[:, :], gps[st.pair][t][:, :], ACT.Square,
                                                        accum_out=w8[:, t:t + 1]), st.done, junk_tok[0])
                    junk_tok[0] = k
                    mix_sq.append(k)
                mix_fg[n] = [dve(lambda e, t=t: e.tensor_tensor(FN[:, t, sl], gps[st.pair][t][:, :], PG[:, sl], ALU.mult),
                                 mix_sq[-2:], S["pg"], na_last) for t in range(2)]
                release(st, *mix_sq[-2:], *mix_fg[n])
                if n == 3:
                    clear(TA)
                    side.append(norm_add("r1", mix_fg, mix_sq, mix_ss, S["xr"], "pre_mlp_g", None))
                return
                yield
            return f

        def ev_up(c, n):
            def f(st):
                while not stage.avail():
                    yield
                i, b, after = stage_get()
                while "r1w" not in S:
                    yield
                z = [act(lambda e, t=t: e.activation(b[:, t], gps[st.pair][t][:, :], ACT.Relu,
                                                     scale=S["r1"][:, t:t + 1]), st.done, S["r1w"], after)
                     for t in range(2)]
                release(st, *z)
                s = dve(lambda e: e.tensor_tensor(b, b, b, ALU.mult), z)
                yield
                yield from turn(b, s, TB, 8 * (c % 2) + 4 * n, free=lambda r: stage.give(i, *r))
            return f

        acc_tok = [None] * 4
        dn_fg, dn_sq = [None] * 4, []
        dn_ss = stat(8)

        def ev_down(c, n):
            def f(st):
                sl = slice(n * 512, (n + 1) * 512)
                if c == 0:
                    acc_tok[n] = [act(lambda e, t=t: e.activation(FN[:, t, sl], gps[st.pair][t][:, :], ACT.Copy),
                                      st.done, S["r1_x"]) for t in range(2)]
                else:
                    acc_tok[n] = [dve(lambda e, t=t: e.tensor_tensor(FN[:, t, sl], FN[:, t, sl], gps[st.pair][t][:, :],
                                                                     ALU.add), st.done, acc_tok[n]) for t in range(2)]
                release(st, *acc_tok[n])
                if c == 1 and n == 0:
                    S["pg2"] = once("d_pg2", sp, PG, d["post_mlp_g"], mix_fg)
                if c == 7:
                    dn_sq.extend(sumsq(FN[:, :, sl], acc_tok[n], dn_ss[:, 2 * n:2 * n + 2]))
                    dn_fg[n] = [dve(lambda e, t=t: e.tensor_tensor(FN[:, t, sl], FN[:, t, sl], PG[:, sl], ALU.mult),
                                    acc_tok[n], dn_sq[-2:], S["pg2"]) for t in range(2)]
                    if n == 3:
                        def spill(cc, ap, w):
                            return once(f"d_x2s{cc}", sp, d["x2s"][cc].rearrange("p (t n) -> p t n", t=2), ap, w)
                        clear(TA)
                        side.append(norm_add("r2", dn_fg, dn_sq, dn_ss, None, "norm_g_2", spill))
                return
                yield
            return f

        SM = PS[:, 80:240].rearrange("p (t n) -> p t n", t=2)
        KROPE = PS[:, 240:368].rearrange("p (t n) -> p t n", t=2)
        CS = PS[:, 368:496].rearrange("p (t n) -> p t n", t=2)
        SN = PS[:, 496:624].rearrange("p (t n) -> p t n", t=2)
        QK2 = ar(4096, 4096).rearrange("p (c n) -> p c n", c=16)
        V2 = ar(8192, 4128).rearrange("p (t h n) -> p t h n", t=2, h=8)
        PRE = Slots([ar(12320 + 518 * i, 518).rearrange("p (k n) -> p k n", k=2) for i in range(2)])
        ROWS = [AR[0:8, 13356 + 256 * i:13612 + 256 * i] for i in range(9)]
        ML_E = Slots([ar(15660 + 384 * i, 384) for i in range(2)])
        ML_S = Slots([ar(16428 + 384 * i, 384) for i in range(2)])

        def angles():
            pf = PS[:, 66:68]
            a = dve(lambda e: e.tensor_copy(pf, POS[:, :]), t_pos)
            ang, kk, red = ROPE_T[0], ROPE_T[1], ROPE_T[2]
            invf = CST[:, C_INVF:C_INVF + 32]
            b = [dve(lambda e, t=t: e.tensor_scalar(ang[:, t], invf, pf[:, t:t + 1], None, ALU.mult), a, t_cst, S["x0_reads"])
                 for t in range(2)]
            yield
            tok = None
            for which in range(2):
                off = 0.25 * which
                m = 12582912.0
                k1 = dve(lambda e, off=off: e.tensor_scalar(kk, ang, float(1 / (2 * np.pi)), off, ALU.mult, ALU.add), b, tok)
                k2 = dve(lambda e: e.tensor_scalar(kk, kk, m, m, ALU.add, ALU.subtract), k1)
                c1, c2 = 6.28125, 1.93500518798828125e-3
                c3 = 2 * np.pi - c1 - c2
                yield
                r1 = dve(lambda e: e.scalar_tensor_tensor(red, kk, -c1, ang, ALU.mult, ALU.add), k2, tok)
                r2 = dve(lambda e: e.scalar_tensor_tensor(red, kk, -c2, red, ALU.mult, ALU.add), r1)
                r3 = dve(lambda e: e.scalar_tensor_tensor(red, kk, -c3, red, ALU.mult, ALU.add), r2)
                lim = 3.1415925
                r4 = dve(lambda e, which=which: e.tensor_scalar(red, red, float(np.pi / 2) * which, lim, ALU.add, ALU.min), r3)
                r5 = dve(lambda e: e.tensor_scalar(red, red, -lim, None, ALU.max), r4)
                yield
                if which == 0:
                    tok = act(lambda e: e.activation(SN[:, :, 32:64], red, ACT.Sin), r5)
                    n1 = dve(lambda e: e.tensor_scalar(SN[:, :, 0:32], SN[:, :, 32:64], -1.0, None, ALU.mult), tok)
                else:
                    tok = act(lambda e: e.activation(CS[:, :, 0:32], red, ACT.Sin), r5)
                    n2 = dve(lambda e: e.tensor_copy(CS[:, :, 32:64], CS[:, :, 0:32]), tok)
                yield
            S["rope"] = [tok, n1, n2]

        ROPE_T = [ar(14576 + 64 * i, 64).rearrange("p (t n) -> p t n", t=2) for i in range(3)]

        row_tok = {}

        def ev_small(st):
            while "r2w" not in S:
                yield
            c = copy_scaled(st, SM, S["r2"], S["r2w"], None)
            release(st, *c)
            S["sm"] = c
            side.append(k_rope())
            yield
            while not banks.avail():
                yield
            j, bk, baft = banks.get()
            for g in range(2):
                for t in range(2):
                    tok = pe(lambda e, g=g, t=t, bk=bk: e.matmul(bk[0:8, g * 256 + t * P:g * 256 + (t + 1) * P],
                                                          SM[:, t, 8 * g:8 * g + 8], ident, start=True, stop=True),
                             c, baft, t_cst)
            yield
            li, fp, ab, lf, F, u, M, en, one = ROWS
            gb = vec("gb", 0, 2, 8)
            w0 = S["r1_x"]
            o = dve(lambda e: e.memset(one, 1.0), S["r2_x"], dn_fg, mix_fg)
            a = dve(lambda e, bk=bk: e.tensor_scalar(li, bk[0:8, 0:256], gb[:, 0:1], None, ALU.add), tok, t_vec, S["r2_x"])
            b = dve(lambda e, bk=bk: e.tensor_scalar(fp, bk[0:8, 256:512], gb[:, 1:2], None, ALU.add), tok, t_vec, S["r2_x"])
            banks.give(j, a, b)
            yield
            c1 = act(lambda e: e.activation(ab, fp, ACT.Abs), b)
            c2 = act(lambda e: e.activation(ab, ab, ACT.Exp, scale=-1.0), c1)
            c3 = act(lambda e: e.activation(ab, ab, ACT.Ln, bias=1.0), c2)
            yield
            e1 = dve(lambda e: e.scalar_tensor_tensor(lf, fp, 0.0, ab, ALU.min, ALU.subtract), c3)
            e2 = dve(lambda e: e.tensor_tensor_scan(F, one, lf, 0.0, ALU.mult, ALU.add), e1, o)
            e3 = dve(lambda e: e.tensor_tensor(u, li, F, ALU.subtract), e2, a)
            e4 = dve(lambda e: e.tensor_tensor_scan(M, u, u, 0.0, ALU.max, ALU.max), e3)
            e5 = dve(lambda e: e.tensor_tensor(en, F, M, ALU.add), e4)
            yield
            x1 = act(lambda e: e.activation(en, en, ACT.Exp, scale=-1.0), e5)
            yield
            while not banks.avail():
                yield
            j, bk, baft = banks.get()
            uN, eN = stat(16), stat(16)
            for g, src in enumerate((u, en)):
                for t in range(2):
                    tok = pe(lambda e, g=g, t=t, src=src, bk=bk: e.matmul(bk[:, 16 * g + 8 * t:16 * g + 8 * t + 8],
                                                                   src[:, t * P:(t + 1) * P], CST[0:8, 0:8],
                                                                   start=True, stop=True), e3, x1, baft, t_cst)
            yield
            c1 = dve(lambda e, bk=bk: e.tensor_copy(uN, bk[:, 0:16]), tok)
            c2 = dve(lambda e, bk=bk: e.tensor_copy(eN, bk[:, 16:32]), tok)
            banks.give(j, c1, c2)
            row_tok.update(uN=uN, eN=eN, w=[c1, c2, e4])

        def k_rope():
            while "rope" not in S:
                yield
            kss = stat(2)
            kr = SM[:, :, 16:80]
            S["kss"], S["kssw"] = kss, sumsq(kr, S["sm"], kss)
            gk = vec("gkr", 0, 64)
            tmp = ar(12320, 256).rearrange("p (a t n) -> p a t n", a=2, t=2)
            tg, ts = tmp[:, 0], tmp[:, 1]
            g = [dve(lambda e, t=t: e.tensor_tensor(tg[:, t], kr[:, t], gk, ALU.mult), S["sm"], t_vec, S["r2_x"],
                     S["r2_reads"]) for t in range(2)]
            yield
            a = dve(lambda e: e.tensor_tensor(ts[:, :, 0:32], tg[:, :, 32:64], SN[:, :, 0:32], ALU.mult), g, S["rope"])
            b = dve(lambda e: e.tensor_tensor(ts[:, :, 32:64], tg[:, :, 0:32], SN[:, :, 32:64], ALU.mult), g, S["rope"])
            c = dve(lambda e: e.tensor_tensor(KROPE, tg, CS, ALU.mult), g, S["rope"])
            yield
            S["krope"] = dve(lambda e: e.tensor_tensor(KROPE, KROPE, ts, ALU.add), a, b, c)

        qk2_ready = [None] * 16
        pre_zero = []

        def ev_qk2(n):
            def f(st):
                while not stage.avail():
                    yield
                i, b, after = stage_get()
                c = copy_scaled(st, b, S["r2"], S["r2w"], after)
                release(st, *c)
                if n == 0:
                    while "krope" not in S:
                        yield
                    for k in range(2):
                        pre_zero.append(dve(lambda e, k=k: e.memset(PRE.bufs[k][:, :, 0:3], 0.0), S["krope"]))
                yield
                for pair in range(2):
                    while not (banks.avail() and PRE.avail()):
                        yield
                    j, bk, baft = banks.get()
                    pi, pre, paft = PRE.get()
                    for k in range(2):
                        for t in range(2):
                            cc = (2 * pair + k) * P
                            tok = pe(lambda e, o=bk[:, k * 256 + t * P:k * 256 + (t + 1) * P], s=b[:, t, cc:cc + P]:
                                     e.transpose(o, s, ident), c, baft, t_cst)
                    yield
                    tk = act(lambda e, bk=bk, pre=pre: e.activation(
                        pre[:, :, 3:259], bk[:, :].rearrange("p (k n) -> p k n", k=2), ACT.Copy), tok, paft, S["krope"])
                    banks.give(j, tk)
                    yield
                    last = [None, None]
                    ct = 4 * n + 2 * pair
                    for m in range(4):
                        for k in range(2):
                            w = vec("conv_w", (ct + k) * 4 + m)
                            s, o = pre[:, k, m:m + 256], QK2[:, ct + k, :]
                            if m == 0:
                                last[k] = dve(lambda e, s=s, o=o, w=w: e.tensor_scalar(o, s, w, None, ALU.mult),
                                              tk, t_vec, pre_zero, S["r2_x"])
                            else:
                                last[k] = dve(lambda e, s=s, o=o, w=w: e.scalar_tensor_tensor(
                                    o, s, w, o, ALU.mult, ALU.add), last[k])
                    yield
                    o2 = QK2[:, ct:ct + 2, :]
                    th = pre[:, :, 3:259]
                    tt = act(lambda e, o2=o2, th=th: e.activation(th, o2, ACT.Tanh, scale=0.5), last)
                    v = dve(lambda e, o2=o2, th=th: e.scalar_tensor_tensor(o2, th, 1.0, o2, ALU.add, ALU.mult), tt)
                    PRE.give(pi, v)
                    qk2_ready[ct] = qk2_ready[ct + 1] = v
                stage.give(i, tok)
            return f

        v2_ready = [None] * 4
        ml_read = []

        def ev_v2(n):
            def f(st):
                w = [S["r2_reads"], S["r2_x"]]
                if n == 0:
                    S["v2one"] = dve(lambda e: e.memset(V2[:, :, :, 256:258], 1.0), w)
                c = [act(lambda e, t=t: e.activation(
                    V2[:, t, 2 * n:2 * n + 2, 0:256], gps[st.pair][t][:, :].rearrange("p (h n) -> p h n", h=2),
                    ACT.Copy, scale=S["r2"][:, t:t + 1]), st.done, S["r2w"], w) for t in range(2)]
                release(st, *c)
                v2_ready[n] = c
                return
                yield
            return f

        oz = {}

        def ev_o(n):
            def f(st):
                while not stage.avail():
                    yield
                i, b, after = stage_get()
                t = tanh_scaled(st, b, S["r2h"], S["r2hw"], after)
                release(st, *t)
                oz["o", n] = (i, b, t)
            return f

        def silu_of(st, done):
            while not stage.avail(2):
                yield
            i, b, after = stage_get()
            i2, b2, after2 = stage_get()
            t = tanh_scaled(st, b, S["r2h"], S["r2hw"], after)
            z = copy_scaled(st, b2, S["r2h"], S["r2hw"], after2)
            release(st, *t, *z)
            s = dve(lambda e: e.scalar_tensor_tensor(b, b, 1.0, b2, ALU.add, ALU.mult), t, z)
            stage.give(i2, s)
            done(i, b, s)

        def ev_z(n):
            def f(st):
                def done(i, b, s):
                    oi, ob, ot = oz["o", n]
                    m = dve(lambda e: e.scalar_tensor_tensor(b, ob, 1.0, b, ALU.add, ALU.mult), s, ot)
                    stage.give(oi, m)
                    oz["oz", n] = (i, b, m)
                yield from silu_of(st, done)
                side.append(ml_pair(n))
            return f

        def ml_pair(n):
            i, b, m = oz["oz", n]
            outs, left = [], [2]
            for h in (2 * n, 2 * n + 1):
                while not (ML_E.avail() and ML_S.avail()):
                    yield
                spawn(ml_head(h, b, m, outs, left))
                for _ in range(3):
                    yield
            while left[0]:
                yield
            yield
            yield from turn(b, outs, TB, 4 * n, ("mlstm_g", 4 * n), free=lambda r: stage.give(i, *r))

        def ml_head(h, ob, om, outs, left):
            ei, E, eaft = ML_E.get()
            si, ST, saft = ML_S.get()
            while not banks.avail(2):
                yield
            j1, f1, a1 = banks.get()
            j2, f2, a2 = banks.get()
            q, k = QK2[:, h, :], QK2[:, 8 + h, :]
            w = [qk2_ready[h], qk2_ready[8 + h], row_tok["w"], S["r2_x"]]
            pe(lambda e: e.matmul(f2[:, 0:256], CST[0:8, h:h + 1].to_broadcast([8, P]), ROWS[6], start=True, stop=True),
               w, a2, t_cst)
            pe(lambda e: e.matmul(f1[:, 0:256], k[:, 0:P], q, start=True, stop=True), w, a1)
            tok = pe(lambda e: e.matmul(f1[:, 256:384], k[:, P:256], q[:, P:256], start=True, stop=True))
            ml_read.append(tok)
            yield
            uN, eN = row_tok["uN"], row_tok["eN"]
            E3 = E.rearrange("p (c n) -> p c n", c=3)
            mk = CST[:, C_MASKT:C_MASKT + P].unsqueeze(1).to_broadcast([P, 2, P])
            a = dve(lambda e: e.tensor_tensor(E3[:, 0:3:2, :], mk, f2[:, 0:256].rearrange("p (c n) -> p c n", c=2),
                                              ALU.subtract), tok, eaft, S["r2_x"])
            x = [act(lambda e: e.activation(E3[:, 1], f2[:, P:256], ACT.Exp, bias=uN[:, h:h + 1], scale=-1.0), a,
                     row_tok["w"], eaft, S["r2_x"]),
                 act(lambda e: e.activation(E3[:, 0], E3[:, 0], ACT.Exp, bias=uN[:, h:h + 1]), a, row_tok["w"]),
                 act(lambda e: e.activation(E3[:, 2], E3[:, 2], ACT.Exp, bias=uN[:, 8 + h:9 + h]), a, row_tok["w"])]
            banks.give(j2, *x, a)
            s = dve(lambda e: e.scalar_tensor_tensor(ST, f1[:, 0:384], float(P ** -0.5) * 0.25, E, ALU.mult, ALU.mult),
                    x, saft)
            banks.give(j1, s)
            ML_E.give(ei, s)
            yield
            yield
            while not banks.avail(2):
                yield
            j1, b1, a1 = banks.get()
            j2, b2, a2 = banks.get()
            vv = v2_ready[h // 2]
            pe(lambda e: e.matmul(b1[:, 0:258], ST[:, 0:P], V2[:, 0, h, :], start=True, stop=True), s, a1, vv, S["v2one"])
            pe(lambda e: e.matmul(b2[:, 0:258], ST[:, P:256], V2[:, 0, h, :], start=True, stop=False), a2)
            tok = pe(lambda e: e.matmul(b2[:, 0:258], ST[:, 256:384], V2[:, 1, h, :], start=False, stop=True))
            ML_S.give(si, tok)
            ml_read.append(tok)
            yield
            dn, ssn, t1, t2, sc = stat(2), stat(2), stat(2), stat(2), stat(2)
            bb = (b1, b2)
            q1 = []
            for t in range(2):
                q1.append(act(lambda e, t=t: e.activation(junk[:, 0:256], bb[t][:, 0:256], ACT.Square,
                                                          accum_out=ssn[:, t:t + 1]), tok, junk_tok[0]))
                junk_tok[0] = q1[-1]
            d0 = [dve(lambda e, t=t: e.tensor_scalar(t1[:, t:t + 1], bb[t][:, 256:257], -1.0,
                                                     eN[:, 8 * t + h:8 * t + h + 1], ALU.mult, ALU.max),
                      q1[t], row_tok["w"]) for t in range(2)]
            d1 = [dve(lambda e, t=t: e.tensor_tensor(dn[:, t:t + 1], bb[t][:, 256:257], t1[:, t:t + 1], ALU.max), d0[t])
                  for t in range(2)]
            d2 = dve(lambda e: e.reciprocal(dn, dn), d1)
            d3 = dve(lambda e: e.tensor_tensor(t1, dn, dn, ALU.mult), d2)
            yield
            d4 = dve(lambda e: e.tensor_tensor(t1, t1, ssn, ALU.mult), d3, q1)
            d5 = dve(lambda e: e.tensor_scalar(t1, t1, 1.0 / 256, 1e-6, ALU.mult, ALU.add), d4)
            pw = pool(lambda e: e.tensor_tensor(t2, t1, half[:, 0:2], ALU.pow), d5, t_half)
            d6 = dve(lambda e: e.scalar_tensor_tensor(sc, dn, 0.5, t2, ALU.mult, ALU.mult), pw)
            yield
            c0 = (h % 2) * 256
            o = [dve(lambda e, t=t: e.scalar_tensor_tensor(ob[:, t, c0:c0 + 256], bb[t][:, 0:256], sc[:, t:t + 1],
                                                           ob[:, t, c0:c0 + 256], ALU.mult, ALU.mult), d6, om, q1)
                 for t in range(2)]
            banks.give(j1, o[0], d1[0])
            banks.give(j2, o[1], d1[1])
            outs.extend(o)
            left[0] -= 1

        ga, spilled = {}, {}

        def ev_ga(n):
            def f(st):
                while not stage.avail():
                    yield
                i, b, after = stage_get()
                t = tanh_scaled(st, b, S["r2h"], S["r2hw"], after)
                release(st, *t)
                ga[n] = (i, b, t)
            return f

        def flat(b):
            return b.rearrange("p t n -> p (t n)")

        def ev_ya(n):
            def f(st):
                i, b, t = ga[n]
                y = [dve(lambda e, t=t: e.scalar_tensor_tensor(b[:, t], b[:, t], 1.0, gps[st.pair][t][:, :], ALU.add,
                                                               ALU.mult), st.done, ga[n][2]) for t in range(2)]
                release(st, *y)
                s = once(f"d_ys{n}", sp, d["ys"][n].rearrange("p (t n) -> p t n", t=2), b, y)
                spilled["y", n] = s
                stage.give(i, s)
                return
                yield
            return f

        HQT = ar(4096, 2048).rearrange("p (c n) -> p c n", c=8)
        HKT = ar(6144, 2048).rearrange("p (c n) -> p c n", c=8)
        HQR = ar(8192, 1024).rearrange("p (c n) -> p c n", c=4)
        HKR = ar(9216, 1024).rearrange("p (c n) -> p c n", c=4)
        HV = ar(10240, 2048).rearrange("p (t n) -> p t n", t=2)
        ZB = [ar(12288 + 1024 * i, 1024).rearrange("p (t n) -> p t n", t=2) for i in range(4)]
        at_p = Slots([ar(16384 + 384 * i, 384) for i in range(2)])
        at_pt = Slots([ar(17152 + 384 * i, 384) for i in range(2)])

        def ev_lat(which):
            def f(st):
                while not stage.avail():
                    yield
                i, b, after = stage_get()
                c = copy_scaled(st, b, S["r2"], S["r2w"], after)
                release(st, *c)
                ss = stat(2)
                q = sumsq(b, c, ss)
                S["lat", which] = rsqrt_of(ss, 2, 1e-6, 1.0 / 512, 2, q)
                yield
                yield from turn(b, c, TB, 8 + 4 * which, ("q_lat_g" if which == 0 else "kv_lat_g", 0),
                                free=lambda r: stage.give(i, *r, *q))
            return f

        zb_tok = {}

        def ev_zb(n):
            def f(st):
                def done(i, b, s):
                    c = dve(lambda e: e.tensor_copy(ZB[n], b), s, ml_read, at_read)
                    stage.give(i, c)
                    zb_tok[n] = c
                yield from silu_of(st, done)
            return f

        def ev_gb(n):
            def f(st):
                while not stage.avail():
                    yield
                i, b, after = stage_get()
                t = tanh_scaled(st, b, S["r2h"], S["r2hw"], after)
                release(st, *t)
                s = once(f"d_gs{n}", sp, d["gs"][n].rearrange("p (t n) -> p t n", t=2), b, t)
                spilled["g", n] = s
                stage.give(i, s)
            return f

        H = {0: dict(nq=0, nk=0, nv=0, qt={}, kt={}, qr=None, kr=None, v={}), 1: dict(nq=0, nk=0, nv=0, qt={}, kt={}, qr=None, kr=None, v={})}
        at_read = []
        ssq = {}
        for hf in range(2):
            H[hf].update(ssq=stat(16).rearrange("p (t h) -> p t h", t=2), ssr=stat(16).rearrange("p (t h) -> p t h", t=2),
                         ssk=stat(16).rearrange("p (t h) -> p t h", t=2), ssqw=[], ssrw=None, rk=[None, None])

        def head_sq(b, c, nh, dst):
            j, sq, after = stage.get()
            s4 = sq.rearrange("p (t n) -> p t n", t=2)
            a = dve(lambda e: e.tensor_tensor(s4, b, b, ALU.mult), c, after)
            r = [dve(lambda e, t=t: e.tensor_reduce(dst[:, t], s4[:, t].rearrange("p (h n) -> p h n", h=nh), AX.X,
                                                    ALU.add), a) for t in range(2)]
            stage.give(j, *r)
            return r

        def to_channels(b, w, dst, c0, scale, war):
            toks = []
            for pair in range(2):
                while not banks.avail():
                    yield
                j, bk, baft = banks.get()
                for k in range(2):
                    for t in range(2):
                        cc = (2 * pair + k) * P
                        tok = pe(lambda e, o=bk[:, k * 256 + t * P:k * 256 + (t + 1) * P], s=b[:, t, cc:cc + P]:
                                 e.transpose(o, s, ident), w, baft, t_cst)
                yield
                o = dst[:, c0 + 2 * pair:c0 + 2 * pair + 2, :]
                s = bk[:, :].rearrange("p (k n) -> p k n", k=2)
                if scale is None:
                    tk = act(lambda e, o=o, s=s: e.activation(o, s, ACT.Copy), tok, war)
                else:
                    tk = act(lambda e, o=o, s=s: e.activation(o, s, ACT.Copy, scale=scale[0]), tok, war, scale[1])
                banks.give(j, tk)
                toks.append(tk)
            return toks, tok

        def ev_uqn(hf, n):
            def f(st):
                while not stage.avail(2):
                    yield
                i, b, after = stage_get()
                c = copy_scaled(st, b, S["lat", 0][0], S["lat", 0][1], after)
                release(st, *c)
                H[hf]["ssqw"] += head_sq(b, c, 4, H[hf]["ssq"][:, :, 4 * n:4 * n + 4])
                yield
                toks, rd = yield from to_channels(b, c, HQT, 4 * n, (S["gqk"], S["gqkw"]), [ml_read, at_read])
                for k in range(4):
                    H[hf]["qt"][4 * n + k] = toks[k // 2]
                stage.give(i, rd, *H[hf]["ssqw"])
            return f

        def ev_uqr(hf):
            def f(st):
                while not stage.avail(3):
                    yield
                i, b, after = stage_get()
                c = copy_scaled(st, b, S["lat", 0][0], S["lat", 0][1], after)
                release(st, *c)
                H[hf]["ssrw"] = head_sq(b, c, 8, H[hf]["ssr"])
                i2, b2, after2 = stage_get()
                yield
                al = []
                for t in range(2):
                    v = b[:, t].rearrange("p (h n) -> p h n", h=8)
                    o = b2[:, t].rearrange("p (h n) -> p h n", h=8)
                    g = vec("gqr", 0, 64).unsqueeze(1).to_broadcast([P, 8, 64])

                    def bc(ap, n):
                        return ap.unsqueeze(1).to_broadcast([P, 8, n])

                    a = dve(lambda e, v=v, g=g: e.tensor_tensor(v, v, g, ALU.mult), c, H[hf]["ssrw"], t_vec)
                    m1 = dve(lambda e, t=t, v=v, o=o: e.tensor_tensor(o[:, :, 0:32], v[:, :, 32:64], bc(SN[:, t, 0:32], 32),
                                                                      ALU.mult), a, after2, S["rope"])
                    m2 = dve(lambda e, t=t, v=v, o=o: e.tensor_tensor(o[:, :, 32:64], v[:, :, 0:32], bc(SN[:, t, 32:64], 32),
                                                                      ALU.mult), a, after2, S["rope"])
                    m3 = dve(lambda e, t=t, v=v: e.tensor_tensor(v, v, bc(CS[:, t], 64), ALU.mult), a, m1, m2, S["rope"])
                    al.append(dve(lambda e, v=v, o=o: e.tensor_tensor(o, o, v, ALU.add), m1, m2, m3))
                stage.give(i, *al)
                yield
                toks, rd = yield from to_channels(b2, al, HQR, 0, None, [ml_read, at_read])
                stage.give(i2, rd)
                H[hf]["qr"] = toks
                while len(H[hf]["ssqw"]) < 4:
                    yield
                tot = stat(16)
                sa = dve(lambda e: e.tensor_tensor(tot.rearrange("p (t h) -> p t h", t=2), H[hf]["ssq"], H[hf]["ssr"], ALU.add),
                         H[hf]["ssqw"], H[hf]["ssrw"])
                r, rw = rsqrt_of(tot, 2, 1e-6, 1.0 / 192, 16, sa)
                w = dve(lambda e: e.tensor_scalar(r, r, float(192 ** -0.5), None, ALU.mult), rw)
                H[hf]["sc"], H[hf]["scw"] = r.rearrange("p (t h) -> p t h", t=2), w
            return f

        def ev_ukn(hf, n):
            def f(st):
                while not stage.avail(2):
                    yield
                i, b, after = stage_get()
                c = copy_scaled(st, b, S["lat", 1][0], S["lat", 1][1], after)
                release(st, *c)
                ssk = H[hf]["ssk"][:, :, 4 * n:4 * n + 4]
                q = head_sq(b, c, 4, ssk)
                tot = stat(8)
                t3 = tot.rearrange("p (t h) -> p t h", t=2)
                a = [dve(lambda e, t=t: e.tensor_scalar(t3[:, t], ssk[:, t], S["kss"][:, t:t + 1], None, ALU.add), q, S["kssw"])
                     for t in range(2)]
                r, rw = rsqrt_of(tot, 2, 1e-6, 1.0 / 192, 8, a)
                H[hf]["rk"][n] = (r.rearrange("p (t h) -> p t h", t=2), rw)
                yield
                yield
                v = b.rearrange("p t (h n) -> p (t h) n", h=4)
                m = dve(lambda e: e.tensor_tensor(v, v, r.unsqueeze(2).to_broadcast([P, 8, P]), ALU.mult), rw, c, q)
                yield
                toks, rd = yield from to_channels(b, m, HKT, 4 * n, None, [ml_read, at_read])
                for k in range(4):
                    H[hf]["kt"][4 * n + k] = toks[k // 2]
                stage.give(i, rd)
                if n == 1:
                    while H[hf]["rk"][0] is None or not stage.avail():
                        yield
                    i, b, after = stage_get()
                    al = []
                    for n2 in range(2):
                        rr, rrw = H[hf]["rk"][n2]
                        for t in range(2):
                            o = b[:, t, 256 * n2:256 * n2 + 256].rearrange("p (h n) -> p h n", h=4)
                            al.append(dve(lambda e, o=o, t=t, rr=rr: e.tensor_tensor(
                                o, KROPE[:, t].unsqueeze(1).to_broadcast([P, 4, 64]),
                                rr[:, t].unsqueeze(2).to_broadcast([P, 4, 64]), ALU.mult), rrw, after, S["krope"]))
                    yield
                    toks, rd = yield from to_channels(b, al, HKR, 0, None, [ml_read, at_read])
                    stage.give(i, rd)
                    H[hf]["kr"] = toks
            return f

        def ev_uv(hf, n):
            def f(st):
                c = copy_scaled(st, HV[:, :, 512 * n:512 * n + 512], S["lat", 1][0], S["lat", 1][1], [ml_read, at_read])
                release(st, *c)
                H[hf]["v"][n] = c
                if n == 1:
                    side.append(at_heads(hf))
                return
                yield
            return f

        def at_heads(hf):
            mine = []
            while H[hf]["kr"] is None or "sc" not in H[hf]:
                yield
            for qd in range(2):
                n = 2 * hf + qd
                while n not in zb_tok or not stage.avail():
                    yield
                i, b, after = stage_get()
                outs, left = [], [4]
                for hh in range(4):
                    while not (at_p.avail() and at_pt.avail()):
                        yield
                    spawn(at_head(hf, 4 * qd + hh, ZB[n], zb_tok[n], b, after, outs, left, mine))
                    for _ in range(2):
                        yield
                while left[0]:
                    yield
                yield
                side.append(turn(b, outs, TB, 4 * n, free=lambda r, i=i: stage.give(i, *r)))
            at_read.extend(mine)
            S["att", hf] = True

        def at_head(hf, h, zb, zw, ob, oaft, outs, left, mine):
            hd = H[hf]
            pi, pb, paft = at_p.get()
            ti, tb, taft = at_pt.get()
            while not banks.avail():
                yield
            j, bk, kaft = banks.get()
            p0, ct = 64 * (h % 2), h // 2
            w = [hd["qt"][h], hd["kt"][h], hd["qr"], hd["kr"], kaft]
            for it, (c0, n) in enumerate(((0, 128), (128, 256))):
                pe(lambda e, it=it, c0=c0, n=n: e.matmul(bk[:, c0:c0 + n], HQT[:, h, it * P:(it + 1) * P],
                                                         HKT[:, h, 0:n], start=True, stop=False), w)
                tok = pe(lambda e, it=it, c0=c0, n=n: e.matmul(bk[:, c0:c0 + n], HQR[p0:p0 + 64, ct, it * P:(it + 1) * P],
                                                               HKR[p0:p0 + 64, ct, 0:n], start=False, stop=True))
            mine.append(tok)
            yield
            mx, nb, sm, rc = stat(2), stat(2), stat(2), stat(2)
            s = dve(lambda e: e.tensor_tensor(pb, bk[:, 0:384], CST[:, C_MASK:C_MASK + 384], ALU.add), tok, paft, t_cst, ml_read)
            banks.give(j, s)
            m = [dve(lambda e: e.tensor_reduce(mx[:, 0:1], pb[:, 0:128], AX.X, ALU.max), s),
                 dve(lambda e: e.tensor_reduce(mx[:, 1:2], pb[:, 128:384], AX.X, ALU.max), s)]
            sc = hd["sc"][:, :, h]
            b = dve(lambda e: e.scalar_tensor_tensor(nb, mx, -1.0, sc, ALU.mult, ALU.mult), m, hd["scw"])
            ex = [act(lambda e, t=t, a=a, z=z: e.activation(pb[:, a:z], pb[:, a:z], ACT.Exp, bias=nb[:, t:t + 1],
                                                            scale=hd["sc"][:, t, h:h + 1], accum_out=sm[:, t:t + 1]), b)
                  for t, (a, z) in enumerate(((0, 128), (128, 384)))]
            yield
            rr = dve(lambda e: e.reciprocal(rc, sm), ex)
            while not banks.avail():
                yield
            j, bk2, kaft = banks.get()
            for c in range(3):
                tok = pe(lambda e, c=c: e.transpose(bk2[:, c * P:(c + 1) * P], pb[:, c * P:(c + 1) * P], ident),
                         ex, kaft, t_cst)
            at_p.give(pi, tok)
            yield
            cp = act(lambda e: e.activation(tb, bk2[:, 0:384], ACT.Copy), tok, taft, ml_read)
            banks.give(j, cp)
            yield
            while not banks.avail():
                yield
            j, bk3, kaft = banks.get()
            vw = hd["v"][h // 4]
            v = HV[:, :, h * P:(h + 1) * P]
            pe(lambda e: e.matmul(bk3[:, 0:P], tb[:, 0:P], v[:, 0], start=True, stop=True), cp, vw, kaft)
            pe(lambda e: e.matmul(bk3[:, P:256], tb[:, P:256], v[:, 0], start=True, stop=False))
            tok = pe(lambda e: e.matmul(bk3[:, P:256], tb[:, 256:384], v[:, 1], start=False, stop=True))
            at_pt.give(ti, tok)
            mine.append(tok)
            yield
            o = [dve(lambda e, t=t: e.scalar_tensor_tensor(
                ob[:, t, (h % 4) * P:(h % 4 + 1) * P], bk3[:, t * P:(t + 1) * P], rc[:, t:t + 1],
                zb[:, t, (h % 4) * P:(h % 4 + 1) * P], ALU.mult, ALU.mult), tok, rr, oaft, zw) for t in range(2)]
            banks.give(j, *o)
            outs.extend(o)
            mine.extend(o)
            left[0] -= 1

        ld_sem = [sem(f"d_ld{i}") for i in range(4)]

        def reload(name, n):
            i, b, after = stage.get()
            src = d[{"y": "ys", "g": "gs", "x": "x2s"}[name]][n]
            w = spilled[name, n] if name != "x" else S["r2_reads"]
            return i, nat(b), dma(sp, b, src, ld_sem[i], w, after)

        def ev_yb(n):
            def f(st):
                while not stage.avail(2):
                    yield
                gi, g, gt = reload("g", n)
                yi, y, yt = reload("y", n)
                m = [dve(lambda e, t=t: e.scalar_tensor_tensor(g[:, t], g[:, t], 1.0, gps[st.pair][t][:, :], ALU.add,
                                                               ALU.mult), st.done, gt) for t in range(2)]
                release(st, *m)
                s = dve(lambda e: e.tensor_tensor(y, y, g, ALU.add), m, yt)
                stage.give(gi, s)
                yield
                if n == 0:
                    clear(TA)
                yield from turn(y, s, TA, 4 * n, scale=0.5, free=lambda r: stage.give(yi, *r))
            return f

        out_sem = [sem(f"d_out{i}") for i in range(4)]
        out_toks = []
        od = out.rearrange("(t p) n -> p t n", p=P)

        def ev_out(n):
            def f(st):
                while not stage.avail():
                    yield
                xi, x, xt = reload("x", n)
                o = [dve(lambda e, t=t: e.tensor_tensor(x[:, t], x[:, t], gps[st.pair][t][:, :], ALU.add), st.done, xt)
                     for t in range(2)]
                release(st, *o)
                s = dma(sp, od[:, :, n * 512:(n + 1) * 512], x, out_sem[n], o)
                out_toks.append(s)
                stage.give(xi, s)
            return f

        for n in range(2):
            Stripe(f"gate{n}", "w_in", 2 + n, 16, TA, 0, ev_gate(n))
            Stripe(f"a{n}", "w_in", n, 16, TA, 0, ev_a(n))
        for n in range(2):
            Stripe(f"q{n}", "w_in", 4 + n, 16, TA, 0, ev_qk(QT1, "q", n))
            Stripe(f"k{n}", "w_in", 6 + n, 16, TA, 0, ev_qk(KT1, "k", n))
            Stripe(f"v{n}", "w_in", 8 + n, 16, TA, 0, ev_v(n))
        mix = [Stripe(f"mix{n}", "w_out", n, 16, TB, 0, ev_mix(n)) for n in range(4)]

        def up(c):
            for n in range(2):
                Stripe(f"up{c}{n}", "w_up", 2 * c + n, 16, TA, 0, ev_up(c, n))

        def down(c):
            for n in range(4):
                Stripe(f"down{c}{n}", "w_down", n, 8, TB, 8 * (c % 2), ev_down(c, n), kfirst=4 * c)

        up(0)
        for c in range(1, 8):
            up(c)
            down(c - 1)
        down(7)
        Stripe("small", "w_small", 0, 16, TA, 0, ev_small, cols=80, per=8)
        for n in range(4):
            Stripe(f"qk2{n}", "w_in_2", n, 16, TA, 0, ev_qk2(n))
        for n in range(4):
            Stripe(f"va{n}", "w_in_2", 4 + n, 16, TA, 0, ev_v2(n))
        for n in range(4):
            Stripe(f"oa{n}", "w_in_2", 8 + n, 16, TA, 0, ev_o(n))
            Stripe(f"za{n}", "w_in_2", 12 + n, 16, TA, 0, ev_z(n))
        for n in range(4):
            Stripe(f"ga{n}", "w_in_2", 22 + n, 16, TA, 0, ev_ga(n))
            Stripe(f"ya{n}", "w_a_2", n, 16, TB, 0, ev_ya(n))
        Stripe("cq", "w_in_2", 16, 16, TA, 0, ev_lat(0))
        Stripe("ckv", "w_in_2", 17, 16, TA, 0, ev_lat(1))
        for n in range(2):
            Stripe(f"zb{n}", "w_in_2", 18 + n, 16, TA, 0, ev_zb(n))

        def latent_up(hf):
            Stripe(f"uqr{hf}", "w_uq_2", 4 + hf, 4, TB, 8, ev_uqr(hf))
            for n in range(2):
                Stripe(f"uqn{hf}{n}", "w_uq_2", 2 * hf + n, 4, TB, 8, ev_uqn(hf, n))
            for n in range(2):
                Stripe(f"ukn{hf}{n}", "w_ukv_2", 2 * hf + n, 4, TB, 12, ev_ukn(hf, n))
            for n in range(2):
                Stripe(f"uv{hf}{n}", "w_ukv_2", 4 + 2 * hf + n, 4, TB, 12, ev_uv(hf, n))

        latent_up(0)
        for n in range(2, 4):
            Stripe(f"zb{n}", "w_in_2", 18 + n, 16, TA, 0, ev_zb(n))
        Stripe("gb0", "w_in_2", 26, 16, TA, 0, ev_gb(0))
        latent_up(1)
        for n in range(1, 4):
            Stripe(f"gb{n}", "w_in_2", 26 + n, 16, TA, 0, ev_gb(n))
        for n in range(4):
            Stripe(f"yb{n}", "w_b_2", n, 16, TB, 0, ev_yb(n))
        for n in range(4):
            Stripe(f"out{n}", "w_out_2", n, 16, TA, 0, ev_out(n))

        def before(st):
            if st.name.startswith("up") and st.name[3] == "0":
                c = int(st.name[2])
                clear(TB, 8 * (c % 2), 8 * (c % 2) + 8)
            if st.name == "oa0":
                clear(TB)
            if st.name == "cq":
                clear(TB, 8, 16)
            if st.name == "zb0":
                S["zb0"] = True
            if st.name == "uqr0":
                clear(TB, 0, 8)
            if st.name == "uqr1":
                until(lambda: ("att", 0) in S, "first half")
            if st.name == "gb1":
                until(lambda: all("kr" in H[1] and len(H[1]["v"]) == 2 for _ in (0,)), "second half")
                clear(TB, 8, 16)

        S["gqk"] = stat(1)
        S["gqkw"] = dve(lambda e: e.tensor_tensor(S["gqk"], vec("gqn"), vec("gkn"), ALU.mult), t_vec)
        for u in range(RAW):
            issue_dma(u)
        g0 = start1()
        side.append(g0)
        for u in range(AHEAD):
            issue_split(u)
            issue_dma(u + RAW)
        for u in range(len(units)):
            issue_split(u + AHEAD)
            issue_dma(u + AHEAD + RAW)
            if units[u]["first"]:
                before(units[u]["st"])
                if units[u]["st"].name == "q0":
                    side.append(angles())
                if units[u]["st"].name == "gate0":
                    until(lambda: "r0hw" in S, "start")
            issue_mm(u)
            advance()
        drain()
        sp(lambda e: e.nop(), out_toks)

        for q in (pe, act, dve, pool, sp):
            q.count()
        block = ctx.enter_context(nc.Block())

        @block.sync
        def _(eng):
            sp.write(eng)

        @block.scalar
        def _(eng):
            act.write(eng)

        @block.vector
        def _(eng):
            dve.write(eng)

        @block.gpsimd
        def _(eng):
            pool.write(eng)

        @block.tensor
        def _(eng):
            pe.write(eng)


def _tiles(w):
    k, n = w.shape
    return w.reshape(k // 256, 2, 128, n // 512, 512).transpose(3, 0, 2, 1, 4).reshape(n // 512, k // 256, 128, 1024)


def _cols(v):
    return v.reshape(-1, 128).T


def kernel(**inputs):
    import concourse.bacc as _bacc
    from concourse import mybir as _mybir
    from concourse.bass_utils import run_bass_kernel_spmd as _run

    g = {k: np.asarray(v) for k, v in inputs.items()}
    A = {}
    A["x"] = g["x"][0]
    A["w_in"] = _tiles(g["w_in"][0])
    A["w_out"] = _tiles(g["w_out"][0])
    A["w_up"] = _tiles(g["w_up"][0])
    A["w_down"] = _tiles(g["w_down"][0])
    w2 = g["w_in_2"][0]
    o = dict(q=0, k=1024, v=2048, o=4096, i=6144, f=6152, z=6160, cq=8208, ckv=8720, kr=9232, zb=9296, ga=11344, gb=13392)
    big = np.concatenate([w2[:, 0:6144], w2[:, o["z"]:o["z"] + 2048], w2[:, o["cq"]:o["cq"] + 1024],
                          w2[:, o["zb"]:o["zb"] + 6144]], axis=1)
    A["w_in_2"] = _tiles(big)
    small = np.concatenate([w2[:, o["i"]:o["i"] + 16], w2[:, o["kr"]:o["kr"] + 64]], axis=1)
    A["w_small"] = small.reshape(2, 8, 128, 80).transpose(0, 2, 1, 3).reshape(2, 128, 640)
    A["w_a_2"] = _tiles(g["w_a_2"][0])
    uq = g["w_uq_2"][0].reshape(512, 16, 192)
    A["w_uq_2"] = _tiles(np.concatenate([uq[:, :, :128].reshape(512, 2048), uq[:, :, 128:].reshape(512, 1024)], axis=1))
    ukv = g["w_ukv_2"][0].reshape(512, 16, 256)
    A["w_ukv_2"] = _tiles(np.concatenate([ukv[:, :, :128].reshape(512, 2048), ukv[:, :, 128:].reshape(512, 2048)], axis=1))
    A["w_b_2"] = _tiles(g["w_b_2"][0])
    A["w_out_2"] = _tiles(g["w_out_2"][0])

    rows, kr = 4, 4
    r, c = np.arange(rows), np.arange(64)
    ridx = np.clip(r - kr // 2, 0, rows - kr)[:, None] + np.arange(kr)[None, :]
    cstart = np.clip(c - 8, 0, 48)
    cmask = (c[None, :] >= cstart[:, None]) & (c[None, :] < cstart[:, None] + 16)
    dr = ridx - r[:, None] + 7
    dc = np.clip(c[None, :] - c[:, None], -15, 15) + 15
    b = g["rpb"][0][:, dr[:, None, :, None], dc[None, :, None, :]]
    b = np.where(cmask[None, None, :, None, :], b, np.float32(NEG)).astype(np.float32)
    A["bias"] = b.reshape(16, 2, 128, 256).transpose(0, 2, 1, 3).reshape(16, 128, 512)

    vecs = np.zeros((128, NVEC), np.float32)

    def put(name, v):
        vecs[0:v.shape[0], VEC[name][0]:VEC[name][0] + v.shape[1]] = v

    put("pre_mix_g", _cols(g["pre_mix_g"][0]))
    put("pre_mlp_g", _cols(g["pre_mlp_g"][0]))
    put("norm_g_2", _cols(g["norm_g_2"][0]))
    put("mlstm_g", _cols(g["mlstm_norm_g_2"][0]))
    put("ln_g", _cols(g["conv_ln_g"][0]))
    put("ln_b", _cols(g["conv_ln_b"][0]))
    put("b_dw", _cols(g["b_dw"][0]))
    put("w_dw", g["w_dw"][0].reshape(31, 8, 128).transpose(2, 1, 0).reshape(128, 248))
    put("conv_w", g["conv_w_2"][0].reshape(4, 16, 128).transpose(2, 1, 0).reshape(128, 64))
    put("q_lat_g", _cols(g["q_lat_g_2"][0]))
    put("kv_lat_g", _cols(g["kv_lat_g_2"][0]))
    put("gqn", g["q_norm_g_2"][0][:128, None])
    put("gkn", g["k_norm_g_2"][0][:128, None])
    put("gqr", np.broadcast_to(g["q_norm_g_2"][0][None, 128:], (128, 64)))
    put("gkr", np.broadcast_to(g["k_norm_g_2"][0][None, 128:], (128, 64)))
    put("gb", g["gate_bias_2"][0].reshape(2, 8).T)
    A["vec"] = vecs
    A["post_mix_g"] = np.broadcast_to(g["post_mix_g"][0][None, :], (128, 2048))
    A["post_mlp_g"] = np.broadcast_to(g["post_mlp_g"][0][None, :], (128, 2048))
    A["pos"] = g["positions_2"][0].astype(np.int32).reshape(2, 128).T

    cst = np.zeros((128, NCST), np.float32)
    cst[:, C_ID:C_ID + 128] = np.eye(128, dtype=np.float32)
    lower = np.where(np.arange(128)[None, :] <= np.arange(128)[:, None], 0.0, NEG).astype(np.float32)
    cst[:, C_MASK:C_MASK + 128] = lower
    cst[:, C_MASK + 256:C_MASK + 384] = lower
    cst[:, C_MASKT:C_MASKT + 128] = lower.T
    cst[:, C_INVF:C_INVF + 32] = np.exp(np.float32(-np.log(10000.0)) * np.arange(0, 64, 2, dtype=np.float32)
                                       / np.float32(64))[None, :]
    A["cst"] = cst

    nc = _bacc.Bacc("TRN2", target_bir_lowering=False, num_devices=1)
    arrays, aps = {}, {}
    for name, a in A.items():
        a = np.ascontiguousarray(a)
        arrays[f"in_{name}"] = a
        aps[name] = nc.dram_tensor(f"in_{name}", a.shape, _mybir.dt.from_np(a.dtype), kind="ExternalInput").ap()
    for name in ("x2s", "ys", "gs"):
        aps[name] = nc.dram_tensor(f"keep_{name}", (4, 128, 1024), F32).ap()
    out = nc.dram_tensor("out_0", (256, 2048), F32, kind="ExternalOutput").ap()
    bass_two_blocks(nc, aps, out)
    res = _run(nc, [arrays], core_ids=[0])
    return np.asarray(res.results[0]["out_0"]).reshape(1, 256, 2048)
```

```python
from contextlib import ExitStack

import numpy as np

import concourse.bass as bass
from concourse import mybir

F32 = mybir.dt.float32
F32R = mybir.dt.float32r
I32 = mybir.dt.int32
ALU = mybir.AluOpType
ACT = mybir.ActivationFunctionType
AX = mybir.AxisListType

P = 128
NB = 512
NEG = -1e30
RAW = 4
RING = 5
AHEAD = RING - 1
SBANKS = 4

VEC = {}
_at = 0
for _name, _n in (("pre_mix_g", 16), ("pre_mlp_g", 16), ("norm_g_2", 16), ("mlstm_g", 16), ("ln_g", 8), ("ln_b", 8),
                  ("b_dw", 8), ("w_dw", 248), ("conv_w", 64), ("q_lat_g", 4), ("kv_lat_g", 4), ("gqn", 1), ("gkn", 1),
                  ("gqr", 64), ("gkr", 64), ("gb", 2)):
    VEC[_name] = (_at, _at + _n)
    _at += _n
NVEC = _at
C_ID, C_MASK, C_MASKT, C_INVF = 0, 128, 512, 640
NCST = 672


class Tok:

    def __init__(self):
        self.sem, self.val, self.used = None, None, False


class Queue:

    def __init__(self, sem):
        self.sem, self.ops = sem, []

    def __call__(self, fn, *waits):
        flat = []
        stack = list(waits)
        while stack:
            w = stack.pop()
            if w is None:
                continue
            if isinstance(w, (list, tuple)):
                stack.extend(w)
            else:
                flat.append(w)
                w.used = True
        t = Tok()
        self.ops.append((fn, flat, t))
        return t

    def count(self):
        n = 0
        for _, _, t in self.ops:
            if t.used and t.sem is None:
                n += 1
                t.sem, t.val = self.sem, n

    def write(self, eng):
        seen = {}
        for fn, waits, t in self.ops:
            need = {}
            for w in waits:
                if need.get(id(w.sem), (None, 0))[1] < w.val:
                    need[id(w.sem)] = (w.sem, w.val)
            for k, (s, v) in need.items():
                if seen.get(k, 0) < v:
                    eng.wait_ge(s, v)
                    seen[k] = v
            ins = fn(eng)
            if t.used and t.sem is self.sem:
                ins.then_inc(self.sem, 1)


class Slots:

    def __init__(self, bufs):
        self.bufs, self.after, self.out, self.at = bufs, [[] for _ in bufs], [False] * len(bufs), 0

    def avail(self, n=1):
        return sum(not o for o in self.out) >= n

    def get(self):
        n = len(self.bufs)
        i = next((self.at + k) % n for k in range(n) if not self.out[(self.at + k) % n])
        self.out[i] = True
        self.at = i + 1
        return i, self.bufs[i], self.after[i]

    def give(self, i, *tokens):
        self.after[i] = list(tokens)
        self.out[i] = False


class TBuf:

    def __init__(self, hi, lo):
        self.hi, self.lo = hi, lo
        self.ready = [None] * 16
        self.read = [[] for _ in range(16)]


def bass_two_blocks(nc, d, out, dbg=None):
    ctx = ExitStack()
    with ctx:
        def sb(name, shape, dt=F32):
            return ctx.enter_context(nc.sbuf_tensor(name, shape, dt))

        def sem(name):
            return ctx.enter_context(nc.semaphore(name))

        raw = [sb(f"raw{i}", [P, 1024]) for i in range(RAW)]
        whi = [sb(f"whi{i}", [P, 1024], F32R) for i in range(RING)]
        wlo = [sb(f"wlo{i}", [P, 1024], F32R) for i in range(RING)]
        TA = TBuf(sb("ta_hi", [P, 16, 256], F32R), sb("ta_lo", [P, 16, 256], F32R))
        TB = TBuf(sb("tb_hi", [P, 16, 256], F32R), sb("tb_lo", [P, 16, 256], F32R))
        AR = sb("arena", [P, 18944])
        STAT = sb("stat", [P, 860])
        PS = sb("ps", [P, 720])
        CST = sb("cst", [P, NCST])
        VC = sb("vc", [P, NVEC])
        POS = sb("pos", [P, 2], I32)
        gps = [[ctx.enter_context(nc.psum_tensor(f"g{p}{t}", [P, NB], F32)) for t in range(2)] for p in range(2)]
        sps = [ctx.enter_context(nc.psum_tensor(f"s{i}", [P, NB], F32)) for i in range(SBANKS)]

        pe, act, dve, pool, sp = (Queue(sem(n)) for n in ("s_pe", "s_act", "s_dve", "s_pool", "s_sp"))
        counts = {}
        pooled = [None]

        def alone(fn, *waits):
            pooled[0] = pool(fn, pooled[0], *waits)
            return pooled[0]

        def dma(q, o, i, s, *waits):
            counts[s.name] = counts.get(s.name, 0) + 16
            q(lambda e: e.dma_start(o, i).then_inc(s, 16), *waits)
            t = Tok()
            t.sem, t.val = s, counts[s.name]
            return t

        def once(name, q, o, i, *waits):
            return dma(q, o, i, sem(name), *waits)

        def ar(a, n):
            return AR[:, a:a + n]

        def vec(name, i=0, n=1, parts=P):
            a = VEC[name][0] + i
            return VC[0:parts, a:a + n]

        ident = CST[:, C_ID:C_ID + P]
        nstat = [0]

        def stat(n):
            a = nstat[0]
            nstat[0] += n
            assert nstat[0] <= 860, nstat[0]
            return STAT[:, a:a + n]

        banks = Slots(sps)
        stage = Slots([ar(1024 * i, 1024) for i in range(4)])
        side = []

        def advance():
            for g in list(side):
                try:
                    next(g)
                except StopIteration:
                    side.remove(g)

        def spawn(g):
            next(g)
            side.append(g)

        def until(cond, what=""):
            n = 0
            while not cond():
                advance()
                n += 1
                assert n < 3000, what

        def pause(n):
            for _ in range(n):
                yield

        def drain():
            until(lambda: not side, "drain")

        def nat(buf, n=512):
            return buf.rearrange("p (t n) -> p t n", t=2) if n == 512 else buf

        t_cst = once("d_cst", act, CST[:, :], d["cst"])
        t_vec = once("d_vec", act, VC[:, :], d["vec"])
        t_pos = once("d_pos", act, POS[:, :], d["pos"])
        half = PS[:, 0:64]
        t_half = alone(lambda e: e.memset(half, -0.5))

        units = []

        class Stripe:
            def __init__(self, name, w, n, kts, T, t0, evac, cols=NB, per=2, kfirst=0):
                self.name, self.evac, self.T, self.cols = name, evac, T, cols
                self.units = []
                for u in range(kts // per):
                    self.units.append(dict(st=self, src=d[w][n, kfirst + u] if w != "w_small" else d[w][u],
                                           kts=[t0 + u * per + k for k in range(per)], first=u == 0,
                                           last=u == kts // per - 1, size=per * cols))
                units.extend(self.units)

        raw_sem = [sem(f"d_raw{i}") for i in range(RAW)]
        raw_tok, hi_tok, lo_tok, mm_tok = {}, {}, {}, {}

        def issue_dma(u):
            if u >= len(units):
                return
            n = units[u]["size"]
            raw_tok[u] = dma(sp, raw[u % RAW][:, 0:n], units[u]["src"], raw_sem[u % RAW],
                             [hi_tok[u - RAW], lo_tok[u - RAW]] if u >= RAW else None)

        def issue_split(u):
            if u >= len(units):
                return
            n = units[u]["size"]
            r, h, l = raw[u % RAW][:, 0:n], whi[u % RING][:, 0:n], wlo[u % RING][:, 0:n]
            hi_tok[u] = act(lambda e: e.activation(h, r, ACT.Copy), raw_tok[u],
                            mm_tok[u - RING] if u >= RING else None)
            plan["dve"] += 1.14 * n / 1024
            lo_tok[u] = dve(lambda e: e.tensor_tensor(l, r, h.bitcast(F32), ALU.subtract), hi_tok[u],
                            mm_tok[u - RING] if u >= RING else None)

        plan = dict(pe=0.0, dve=0.0)

        def busy():
            plan["dve"] = max(plan["dve"], plan["pe"] - 1.0)
            return plan["dve"] > plan["pe"] + 2.0

        gfree = [[], []]
        nstripe = [0]

        def issue_mm(u):
            un = units[u]
            st, T, c = un["st"], un["st"].T, un["st"].cols
            if st.name == "small":
                return issue_small(u)
            if un["first"]:
                st.pair = nstripe[0] % 2
                nstripe[0] += 1
                until(lambda: gfree[st.pair] is not None, st.name + " psum")
                st.free, gfree[st.pair] = gfree[st.pair], None
            for kt in un["kts"]:
                until(lambda: T.ready[kt] is not None, f"{st.name} kt {kt}")
            first_wait = [hi_tok[u], lo_tok[u], st.free if un["first"] else None]
            for j, kt in enumerate(un["kts"]):
                wh = whi[u % RING][:, j * c:(j + 1) * c]
                wl = wlo[u % RING][:, j * c:(j + 1) * c]
                for t in range(2):
                    o = gps[st.pair][t][:, 0:c]
                    xh, xl = T.hi[:, kt, t * P:(t + 1) * P], T.lo[:, kt, t * P:(t + 1) * P]
                    a = un["first"] and j == 0
                    z = un["last"] and j == len(un["kts"]) - 1
                    pe(lambda e, o=o, x=xh, w=wh, a=a: e.matmul(o, x, w, start=a, stop=False),
                       first_wait, T.ready[kt])
                    first_wait = None
                    pe(lambda e, o=o, x=xh, w=wl: e.matmul(o, x, w, start=False, stop=False))
                    tok = pe(lambda e, o=o, x=xl, w=wh, z=z: e.matmul(o, x, w, start=False, stop=z))
                T.read[kt] = [tok]
                plan["pe"] += 1.29
                if j + 1 < len(un["kts"]) and un["st"].cols == NB:
                    advance()
            mm_tok[u] = tok
            if un["last"]:
                st.done = tok
                side.append(st.evac(st))

        def issue_small(u):
            un = units[u]
            st, T, c = un["st"], un["st"].T, un["st"].cols
            if un["first"]:
                st.pair = nstripe[0] % 2
                nstripe[0] += 1
                until(lambda: gfree[st.pair] is not None, st.name + " psum")
                st.free, gfree[st.pair] = gfree[st.pair], None
            o = gps[st.pair][0][0:c, 0:256]
            wait = [hi_tok[u], lo_tok[u], st.free if un["first"] else None]
            for j, kt in enumerate(un["kts"]):
                wh = whi[u % RING][:, j * c:(j + 1) * c]
                wl = wlo[u % RING][:, j * c:(j + 1) * c]
                a, z = un["first"] and j == 0, un["last"] and j == len(un["kts"]) - 1
                pe(lambda e, w=wh, kt=kt, a=a: e.matmul(o, w, T.hi[:, kt, :], start=a, stop=False), wait, T.ready[kt])
                pe(lambda e, w=wl, kt=kt: e.matmul(o, w, T.hi[:, kt, :], start=False, stop=False))
                tok = pe(lambda e, w=wh, kt=kt, z=z: e.matmul(o, w, T.lo[:, kt, :], start=False, stop=z))
                T.read[kt] = [tok]
                plan["pe"] += 0.33
            mm_tok[u] = tok
            if un["last"]:
                st.done = tok
                side.append(st.evac(st))

        def release(st, *tokens):
            gfree[st.pair] = list(tokens)

        def rsqrt_of(ss, n, eps, scale, w, *waits):
            v, r = stat(w), stat(w)
            a = dve(lambda e: e.tensor_scalar(v, ss, scale, eps, ALU.mult, ALU.add), *waits)
            b = alone(lambda e: e.tensor_tensor(r, v, half[:, 0:w], ALU.pow), a, t_half)
            return r, b

        def turn(src, srcw, T, kt0, g=None, scale=None, free=None):
            reads = []
            for pair in range(2):
                while not banks.avail():
                    yield
                i, b, after = banks.get()
                for k in range(2):
                    for t in range(2):
                        c = (2 * pair + k) * P
                        tok = pe(lambda e, o=b[:, k * 256 + t * P:k * 256 + (t + 1) * P], s=src[:, t, c:c + P]:
                                 e.transpose(o, s, ident), srcw, after, t_cst)
                reads.append(tok)
                if pair == 1 and free is not None:
                    free(reads)
                yield
                kt = kt0 + 2 * pair
                war = [T.read[kt], T.read[kt + 1]]
                if g is None:
                    h, l = T.hi[:, kt:kt + 2, :], T.lo[:, kt:kt + 2, :]
                    s = b[:, :].rearrange("p (k n) -> p k n", k=2)
                    if scale is None:
                        a = act(lambda e, h=h, s=s: e.activation(h, s, ACT.Copy), tok, war)
                        v = dve(lambda e, h=h, l=l, s=s: e.tensor_tensor(l, s, h.bitcast(F32), ALU.subtract), a, war)
                    else:
                        a = act(lambda e, h=h, s=s: e.activation(h, s, ACT.Copy, scale=scale), tok, war)
                        v = dve(lambda e, h=h, l=l, s=s: e.scalar_tensor_tensor(l, s, scale, h.bitcast(F32), ALU.mult,
                                                                                ALU.subtract), a, war)
                    T.ready[kt] = T.ready[kt + 1] = [a, v]
                    banks.give(i, a, v)
                else:
                    al = []
                    for k in range(2):
                        h, s = T.hi[:, kt + k, :], b[:, k * 256:(k + 1) * 256]
                        gg = vec(g[0], g[1] + 2 * pair + k)
                        a = act(lambda e, h=h, s=s, gg=gg: e.activation(h, s, ACT.Copy, scale=gg), tok, war, t_vec)
                    for k in range(2):
                        h, l, s = T.hi[:, kt + k, :], T.lo[:, kt + k, :], b[:, k * 256:(k + 1) * 256]
                        gg = vec(g[0], g[1] + 2 * pair + k)
                        v = dve(lambda e, h=h, l=l, s=s, gg=gg: e.scalar_tensor_tensor(
                            l, s, gg, h.bitcast(F32), ALU.mult, ALU.subtract), a, war, t_vec)
                        T.ready[kt + k] = [a, v]
                        al += [a, v]
                    banks.give(i, *al)

        def clear(T, a=0, b=16):
            for k in range(a, b):
                T.ready[k] = None

        def copy_scaled(st, dst, r, rw, waits):
            return [act(lambda e, t=t: e.activation(dst[:, t], gps[st.pair][t][:, 0:dst.shape[2]], ACT.Copy,
                                                    scale=r[:, t:t + 1]), st.done, rw, waits) for t in range(2)]

        def tanh_scaled(st, dst, r, rw, waits):
            return [act(lambda e, t=t: e.activation(dst[:, t], gps[st.pair][t][:, :], ACT.Tanh,
                                                    scale=r[:, t:t + 1]), st.done, rw, waits) for t in range(2)]

        def stage_get():
            i, b, after = stage.get()
            return i, nat(b), after

        def sumsq(src, waits, w):
            toks = []
            for t in range(2):
                toks.append(act(lambda e, t=t: e.activation(junk[:, 0:src.shape[2]], src[:, t], ACT.Square,
                                                            accum_out=w[:, t:t + 1]),
                                waits[t] if isinstance(waits, list) else waits, junk_tok[0]))
                junk_tok[0] = toks[-1]
            return toks

        junk = sb("junk", [P, 512])
        junk_tok = [None]

        def halved(r, rw):
            h = stat(2)
            return h, dve(lambda e: e.tensor_scalar(h, r, 0.5, None, ALU.mult), rw)

        S = {}
        X0 = ar(4096, 4096).rearrange("p (t n) -> p t n", t=2)
        QT1 = ar(4096, 2048).rearrange("p (c n) -> p c n", c=8)
        KT1 = ar(6144, 2048).rearrange("p (c n) -> p c n", c=8)
        V1 = ar(8192, 2048).rearrange("p (t n) -> p t n", t=2)
        UT = ar(10240, 2288).rearrange("p (c n) -> p c n", c=8)
        CV = ar(12528, 2048).rearrange("p (c n) -> p c n", c=8)
        LNN = ar(10240, 2048).rearrange("p (t n) -> p t n", t=2)
        na_p = Slots([ar(14576 + 512 * i, 512) for i in range(4)])
        na_pt = Slots([ar(16624 + 512 * i, 512) for i in range(2)])
        na_km = Slots([ar(17648 + 512 * i, 512) for i in range(2)])
        na_bias_sem = [sem(f"d_bias{i}") for i in range(4)]
        xd = d["x"].rearrange("(t p) n -> p t n", p=P)

        ld = []

        def load_x():
            c = len(ld)
            ld.append(once(f"d_x{c}", sp, X0[:, :, c * 512:(c + 1) * 512], xd[:, :, c * 512:(c + 1) * 512]))

        def start1():
            ss4 = stat(8)
            S["x0_reads"] = []
            sq = []
            for c in range(4):
                yield from turn(X0[:, :, c * 512:(c + 1) * 512], ld[c], TA, 4 * c, ("pre_mix_g", 4 * c),
                                free=S["x0_reads"].extend)
                sq += sumsq(X0[:, :, c * 512:(c + 1) * 512], ld[c], ss4[:, 2 * c:2 * c + 2])
            S["x0_reads"] += sq
            ss = stat(2)
            a = dve(lambda e: e.tensor_reduce(ss, ss4.rearrange("p (c t) -> p t c", t=2), AX.X, ALU.add), sq)
            r, rw = rsqrt_of(ss, 2, 1e-6, 1.0 / 2048, 2, a)
            S["r0"], S["r0w"] = r, rw
            S["r0h"], S["r0hw"] = halved(r, rw)

        gate_buf = {}
        t_upad = [dve(lambda e: e.memset(UT[:, :, 0:15], 0.0)), dve(lambda e: e.memset(UT[:, :, 271:286], 0.0))]
        conv_ready = [None] * 8

        def ev_gate(n):
            def f(st):
                while not stage.avail() or "r0hw" not in S:
                    yield
                i, b, after = stage_get()
                t = tanh_scaled(st, b, S["r0h"], S["r0hw"], after)
                release(st, *t)
                gate_buf[n] = (i, b, t)
            return f

        def ev_a(n):
            def f(st):
                while not stage.avail():
                    yield
                i, b, after = stage_get()
                c = copy_scaled(st, b, S["r0h"], S["r0hw"], after)
                release(st, *c)
                gi, gb, gt = gate_buf.pop(n)
                u = dve(lambda e: e.scalar_tensor_tensor(b, gb, 1.0, b, ALU.add, ALU.mult), c, gt)
                stage.give(gi, u)
                yield from pause(6)
                for pair in range(2):
                    while not banks.avail():
                        yield
                    j, bk, baft = banks.get()
                    for k in range(2):
                        for t in range(2):
                            cc = (2 * pair + k) * P
                            tok = pe(lambda e, o=bk[:, k * 256 + t * P:k * 256 + (t + 1) * P], s=b[:, t, cc:cc + P]:
                                     e.transpose(o, s, ident), u, baft, t_cst)
                    yield
                    ct = 4 * n + 2 * pair
                    tk = act(lambda e, ct=ct, bk=bk: e.activation(
                        UT[:, ct:ct + 2, 15:271], bk[:, :].rearrange("p (k n) -> p k n", k=2), ACT.Copy), tok)
                    banks.give(j, tk)
                    conv_ready[ct] = conv_ready[ct + 1] = tk
                stage.give(i, tok)
                if n == 0:
                    side.append(conv())
            return f

        conv_done = [None] * 8

        def conv():
            for n in range(2):
                cts = range(4 * n, 4 * n + 4)
                while any(conv_ready[ct] is None for ct in cts):
                    yield
                last = {}
                for j in range(31):
                    for ct in cts:
                        while busy():
                            yield
                        plan["dve"] += 0.36
                        w = vec("w_dw", ct * 31 + j)
                        src, dst = UT[:, ct, j:j + 256], CV[:, ct, :]
                        if j == 0:
                            last[ct] = act(lambda e, w=w, s=src, o=dst, ct=ct: e.activation(
                                o, s, ACT.Identity, scale=w, bias=vec("b_dw", ct)), conv_ready[ct], t_vec, t_upad)
                        else:
                            last[ct] = dve(lambda e, w=w, s=src, o=dst: e.scalar_tensor_tensor(
                                o, s, w, o, ALU.mult, ALU.add), last[ct])
                for ct in cts:
                    conv_done[ct] = last[ct]
            yield from conv_ln()

        LN_PAUSE = 2

        def conv_ln():
            while any(c is None for c in conv_done):
                yield
            yield from pause(LN_PAUSE)
            st6 = [stat(12), stat(12)]
            mv = [stat(2), stat(2)]
            var = stat(2)
            cp, bn = [[], []], [[], []]
            for t in range(2):
                for hf in range(2):
                    while not banks.avail():
                        yield
                    j, bk, baft = banks.get()
                    for k in range(4):
                        tok = pe(lambda e, o=bk[:, k * P:(k + 1) * P], s=CV[:, 4 * hf + k, t * P:(t + 1) * P]:
                                 e.transpose(o, s, ident), conv_done, baft, t_cst)
                    yield
                    a = act(lambda e, t=t, hf=hf, bk=bk: e.activation(
                        LNN[:, t, hf * 512:(hf + 1) * 512], bk[:, :], ACT.Copy), tok, conv_done)
                    v = dve(lambda e, t=t, hf=hf, bk=bk: e.bn_stats(st6[t][:, 6 * hf:6 * hf + 6], bk[:, :]), a)
                    banks.give(j, a, v)
                    cp[t].append(a)
                    bn[t].append(v)
            ag = [dve(lambda e, t=t: e.bn_aggr(mv[t], st6[t].rearrange("p (a b) -> p a b", a=2)), bn[t])
                  for t in range(2)]
            yield
            vv = [dve(lambda e, t=t: e.tensor_scalar(var[:, t:t + 1], mv[t][:, 1:2], 1e-5, None, ALU.add), ag[t])
                  for t in range(2)]
            rs = stat(2)
            pw = alone(lambda e: e.tensor_tensor(rs, var, half[:, 0:2], ALU.pow), vv, t_half)
            yield
            nm = [dve(lambda e, t=t: e.tensor_scalar(LNN[:, t], LNN[:, t], mv[t][:, 0:1], rs[:, t:t + 1],
                                                     ALU.subtract, ALU.mult), pw, cp[t]) for t in range(2)]
            yield
            yield
            for pair in range(4):
                while not (banks.avail() and stage.avail()):
                    yield
                j, bk, baft = banks.get()
                i, zb, zaft = stage.get()
                for k in range(2):
                    for t in range(2):
                        cc = (2 * pair + k) * P
                        tok = pe(lambda e, o=bk[:, k * 256 + t * P:k * 256 + (t + 1) * P], s=LNN[:, t, cc:cc + P]:
                                 e.transpose(o, s, ident), nm, baft, t_cst)
                S["ln_reads"] = tok
                yield
                z, th = zb[:, 0:512], zb[:, 512:1024]
                za = [act(lambda e, k=k, bk=bk, z=z, ct=2 * pair + k: e.activation(
                    z[:, k * 256:(k + 1) * 256], bk[:, k * 256:(k + 1) * 256], ACT.Identity,
                    scale=vec("ln_g", ct), bias=vec("ln_b", ct)), tok, zaft, t_vec) for k in range(2)]
                banks.give(j, *za)
                ta = act(lambda e, z=z, th=th: e.activation(th, z, ACT.Tanh, scale=0.5), za)
                y = dve(lambda e, z=z, th=th: e.scalar_tensor_tensor(z, th, 1.0, z, ALU.add, ALU.mult), ta)
                yield
                kt = 2 * pair
                war = [TB.read[kt], TB.read[kt + 1]]
                h, l = TB.hi[:, kt:kt + 2, :], TB.lo[:, kt:kt + 2, :]
                s = z.rearrange("p (k n) -> p k n", k=2)
                a = act(lambda e, h=h, s=s: e.activation(h, s, ACT.Copy, scale=0.5), y, war)
                v = dve(lambda e, h=h, l=l, s=s: e.scalar_tensor_tensor(l, s, 0.5, h.bitcast(F32), ALU.mult,
                                                                        ALU.subtract), a, war)
                TB.ready[kt] = TB.ready[kt + 1] = [a, v]
                stage.give(i, a, v)

        qk_ready = {}

        def ev_qk(dst, key, n):
            def f(st):
                while not stage.avail():
                    yield
                i, b, after = stage_get()
                c = copy_scaled(st, b, S["r0"], S["r0w"], after)
                release(st, *c)
                yield from pause(2)
                for pair in range(2):
                    while not banks.avail():
                        yield
                    j, bk, baft = banks.get()
                    for k in range(2):
                        for t in range(2):
                            cc = (2 * pair + k) * P
                            tok = pe(lambda e, o=bk[:, k * 256 + t * P:k * 256 + (t + 1) * P], s=b[:, t, cc:cc + P]:
                                     e.transpose(o, s, ident), c, baft, t_cst)
                    yield
                    ct = 4 * n + 2 * pair
                    tk = act(lambda e, ct=ct, bk=bk: e.activation(
                        dst[:, ct:ct + 2, :], bk[:, :].rearrange("p (k n) -> p k n", k=2), ACT.Copy,
                        scale=0.125 if key == "q" else 1.0), tok, S["x0_reads"])
                    banks.give(j, tk)
                    qk_ready[key, ct] = qk_ready[key, ct + 1] = tk
                stage.give(i, tok)
            return f

        v_ready = {}

        def ev_v(n):
            def f(st):
                c = copy_scaled(st, V1[:, :, n * 512:(n + 1) * 512], S["r0"], S["r0w"], None)
                release(st, *c)
                v_ready[n] = c
                side.append(na_heads(n))
                return
                yield
            return f

        na_out = {}

        t_km = [alone(lambda e, b=b, p=p, c=c: e.memset(b[p:p + 64, c:c + 256], 0.0))
                for b in na_km.bufs for p, c in ((64, 0), (0, 256))]

        NA_PACE = (5, 4)
        NA_PAUSE = (4, 3)

        def na_heads(n):
            while not stage.avail():
                yield
            i, b, after = stage_get()
            left = [8]
            outs = []
            for pr in range(4 * n, 4 * n + 4):
                while not na_km.avail() or ("q", pr) not in qk_ready or ("k", pr) not in qk_ready:
                    yield
                ki, km, kaft = na_km.get()
                kc = [alone(lambda e, km=km, pr=pr, p=p, c=c: e.tensor_copy(km[p:p + 64, c:c + 256], KT1[p:p + 64, pr, :]),
                           qk_ready["k", pr], kaft, t_km) for p, c in ((0, 0), (64, 256))]
                qk = []
                for it in range(2):
                    while not na_p.avail():
                        yield
                    spawn(na_item(pr, it, km, kc, b, after, outs, left, qk))
                    yield from pause(NA_PACE[n])
                while len(qk) < 2:
                    yield
                na_km.give(ki, *qk)
            while left[0]:
                yield
            yield from turn(b, outs, TB, 8 + 4 * n, free=lambda r: stage.give(i, *r))

        na_last, na_qk = [], []

        def na_item(pr, it, km, kc, ob, oaft, outs, left, qk):
            on_pe = pr < 4
            plan["dve"] += 0.9 if on_pe else 1.6
            plan["pe"] += 2.6 if on_pe else 2.2
            pi, pb, paft = na_p.get()
            bl = dma(pool, pb, d["bias"][pr, it], na_bias_sem[pi], paft)
            yield
            while not banks.avail():
                yield
            j, bk, kaft = banks.get()
            tok = pe(lambda e: e.matmul(bk[:, :], QT1[:, pr, it * P:(it + 1) * P], km, start=True, stop=not on_pe),
                     qk_ready["q", pr], kc, kaft)
            if on_pe:
                tok = pe(lambda e: e.matmul(bk[:, :], ident, pb, start=False, stop=True), bl)
            qk.append(tok)
            na_qk.append(tok)
            yield from pause(2)
            mx, sm, rc = stat(2), stat(2), stat(2)
            s3, p3 = (v.rearrange("p (h n) -> p h n", h=2) for v in (bk[:, :], pb))
            if not on_pe:
                tok = dve(lambda e: e.tensor_tensor(pb, bk[:, :], pb, ALU.add), tok, bl)
                banks.give(j, tok)
                s3 = p3
            m = dve(lambda e: e.tensor_reduce(mx, s3, AX.X, ALU.max, negate=True), tok)
            ex = [act(lambda e, h=h: e.activation(p3[:, h], s3[:, h], ACT.Exp, bias=mx[:, h:h + 1],
                                                  accum_out=sm[:, h:h + 1]), m) for h in range(2)]
            if on_pe:
                banks.give(j, *ex)
            yield from pause(NA_PAUSE[0 if on_pe else 1])
            rr = dve(lambda e: e.reciprocal(rc, sm), ex)
            while not (banks.avail() and na_pt.avail()):
                yield
            j, bk2, kaft = banks.get()
            ti, tb, taft = na_pt.get()
            for c in range(4):
                tok = pe(lambda e, c=c: e.transpose(bk2[:, c * P:(c + 1) * P], pb[:, c * P:(c + 1) * P], ident),
                         ex, kaft, t_cst)
            na_p.give(pi, tok)
            yield
            cp = act(lambda e: e.activation(tb, bk2[:, :], ACT.Copy), tok, taft)
            banks.give(j, cp)
            yield
            while not banks.avail():
                yield
            j, bk3, kaft = banks.get()
            for h in range(2):
                for jt in range(2):
                    tok = pe(lambda e, h=h, jt=jt: e.matmul(
                        bk3[:, h * P:(h + 1) * P], tb[:, h * 256 + jt * P:h * 256 + (jt + 1) * P],
                        V1[:, jt, pr * P:(pr + 1) * P], start=jt == 0, stop=jt == 1), cp, v_ready[pr // 4], kaft)
            na_pt.give(ti, tok)
            na_last.append(tok)
            yield
            c0 = (pr % 4) * P
            o = [act(lambda e, h=h: e.activation(ob[:, it, c0 + 64 * h:c0 + 64 * h + 64],
                                                 bk3[:, h * P + 64 * h:h * P + 64 * h + 64], ACT.Copy,
                                                 scale=rc[:, h:h + 1]), tok, rr, oaft) for h in range(2)]
            banks.give(j, *o)
            outs.extend(o)
            left[0] -= 1

        FN = ar(10240, 4096).rearrange("p (t n) -> p t n", t=2)
        XR = ar(4096, 4096).rearrange("p (t n) -> p t n", t=2)
        PG = ar(8192, 2048)

        def norm_add(key, fg, last_gain, sq, ss4, xw, gname, after_x):
            ss = stat(2)
            a = dve(lambda e: e.tensor_reduce(ss, ss4.rearrange("p (c t) -> p t c", t=2), AX.X, ALU.add), sq)
            r, rw = rsqrt_of(ss, 2, 1e-6, 1.0 / 2048, 2, a)
            last_gain()
            xs4 = stat(8)
            xsq, reads = [], []

            def add(c):
                sl = slice(c * 512, (c + 1) * 512)
                return [dve(lambda e, t=t: e.scalar_tensor_tensor(
                    XR[:, t, sl], FN[:, t, sl], r[:, t:t + 1], XR[:, t, sl], ALU.mult, ALU.add), rw, fg[c], xw)
                    for t in range(2)]

            ad = {0: add(0)}
            for c in range(4):
                if c < 3:
                    ad[c + 1] = add(c + 1)
                yield from turn(XR[:, :, c * 512:(c + 1) * 512], ad[c], TA, 4 * c, (gname, 4 * c), free=reads.extend)
            for c in range(4):
                xc = XR[:, :, c * 512:(c + 1) * 512]
                xsq += sumsq(xc, ad[c], xs4[:, 2 * c:2 * c + 2])
                if after_x is not None:
                    reads.append(after_x(c, xc, ad[c]))
                yield
            S[key + "_x"] = ad[3]
            S[key + "_reads"] = reads + xsq
            sx = stat(2)
            a = dve(lambda e: e.tensor_reduce(sx, xs4.rearrange("p (c t) -> p t c", t=2), AX.X, ALU.add), xsq)
            rx, rxw = rsqrt_of(sx, 2, 1e-6, 1.0 / 2048, 2, a)
            S[key], S[key + "w"] = rx, rxw
            S[key + "h"], S[key + "hw"] = halved(rx, rxw)

        mix_fg, mix_sq = [None] * 4, []
        mix_ss = stat(8)

        def ev_mix0(n):
            def f(st):
                sl = slice(n * 512, (n + 1) * 512)
                mix_fg[n] = [act(lambda e, t=t: e.activation(FN[:, t, sl], gps[st.pair][t][:, :], ACT.Copy),
                                 st.done, TB.ready[0:8], conv_done, S["ln_reads"]) for t in range(2)]
                release(st, *mix_fg[n])
                return
                yield
            return f

        def ev_mix1(n):
            def f(st):
                sl = slice(n * 512, (n + 1) * 512)
                if n == 0:
                    S["xr"] = [once(f"d_xr{c}", pool, XR[:, :, c * 512:(c + 1) * 512], xd[:, :, c * 512:(c + 1) * 512],
                                    na_qk) for c in range(4)]
                    S["pg"] = once("d_pg", pool, PG, d["post_mix_g"], na_last)
                ad = [dve(lambda e, t=t: e.tensor_tensor(FN[:, t, sl], FN[:, t, sl], gps[st.pair][t][:, :], ALU.add),
                          st.done, mix_fg[n]) for t in range(2)]
                release(st, *ad)
                mix_sq.extend(sumsq(FN[:, :, sl], ad, mix_ss[:, 2 * n:2 * n + 2]))

                def gain():
                    mix_fg[n] = [dve(lambda e, t=t: e.tensor_tensor(FN[:, t, sl], FN[:, t, sl], PG[:, sl], ALU.mult),
                                     ad, mix_sq[2 * n:2 * n + 2], S["pg"]) for t in range(2)]

                if n < 3:
                    gain()
                else:
                    clear(TA)
                    yield from norm_add("r1", mix_fg, gain, mix_sq, mix_ss, S["xr"], "pre_mlp_g", None)
            return f

        def ev_up(c, n):
            def f(st):
                while not stage.avail():
                    yield
                i, b, after = stage_get()
                while "r1w" not in S:
                    yield
                z = [act(lambda e, t=t: e.activation(b[:, t], gps[st.pair][t][:, :], ACT.Relu,
                                                     scale=S["r1"][:, t:t + 1]), st.done, S["r1w"], after)
                     for t in range(2)]
                release(st, *z)
                s = dve(lambda e: e.tensor_tensor(b, b, b, ALU.mult), z)
                yield from pause(3)
                yield from turn(b, s, TB, 8 * (c % 2) + 4 * n, free=lambda r: stage.give(i, *r))
            return f

        acc_tok = [None] * 4
        dn_fg, dn_sq = [None] * 4, []
        dn_ss = stat(8)

        def ev_down(c, n):
            def f(st):
                sl = slice(n * 512, (n + 1) * 512)
                if c == 0:
                    acc_tok[n] = [act(lambda e, t=t: e.activation(FN[:, t, sl], gps[st.pair][t][:, :], ACT.Copy),
                                      st.done, S["r1_x"]) for t in range(2)]
                    if n == 0:
                        side.append(angles())
                else:
                    acc_tok[n] = [dve(lambda e, t=t: e.tensor_tensor(FN[:, t, sl], FN[:, t, sl], gps[st.pair][t][:, :],
                                                                     ALU.add), st.done, acc_tok[n]) for t in range(2)]
                release(st, *acc_tok[n])
                if c == 1 and n == 0:
                    S["pg2"] = once("d_pg2", sp, PG, d["post_mlp_g"], mix_fg)
                if c == 7:
                    dn_sq.extend(sumsq(FN[:, :, sl], acc_tok[n], dn_ss[:, 2 * n:2 * n + 2]))

                    def gain():
                        dn_fg[n] = [dve(lambda e, t=t: e.tensor_tensor(FN[:, t, sl], FN[:, t, sl], PG[:, sl], ALU.mult),
                                        acc_tok[n], dn_sq[2 * n:2 * n + 2], S["pg2"]) for t in range(2)]

                    if n < 3:
                        gain()
                    else:
                        def spill(cc, ap, w):
                            return once(f"d_x2s{cc}", sp, d["x2s"][cc].rearrange("p (t n) -> p t n", t=2), ap, w)
                        clear(TA)
                        yield from norm_add("r2", dn_fg, gain, dn_sq, dn_ss, None, "norm_g_2", spill)
            return f

        SM = PS[:, 80:240].rearrange("p (t n) -> p t n", t=2)
        KROPE = PS[:, 240:368].rearrange("p (t n) -> p t n", t=2)
        CS = PS[:, 368:496].rearrange("p (t n) -> p t n", t=2)
        SN = PS[:, 496:624].rearrange("p (t n) -> p t n", t=2)
        QK2 = ar(4096, 4096).rearrange("p (c n) -> p c n", c=16)
        V2 = ar(8192, 4128).rearrange("p (t h n) -> p t h n", t=2, h=8)
        PRE = Slots([ar(12320 + 518 * i, 518).rearrange("p (k n) -> p k n", k=2) for i in range(2)])
        ROWS = [AR[0:8, 13356 + 256 * i:13612 + 256 * i] for i in range(9)]
        ML_E = Slots([ar(15660 + 384 * i, 384) for i in range(2)])
        ML_S = Slots([ar(16428 + 384 * i, 384) for i in range(2)])

        def angles():
            pf = PS[:, 66:68]
            a = dve(lambda e: e.tensor_copy(pf, POS[:, :]), t_pos)
            ang, kk, red = ROPE_T[0], ROPE_T[1], ROPE_T[2]
            invf = CST[:, C_INVF:C_INVF + 32]
            b = [dve(lambda e, t=t: e.tensor_scalar(ang[:, t], invf, pf[:, t:t + 1], None, ALU.mult), a, t_cst, na_last)
                 for t in range(2)]
            yield
            tok = None
            for which in range(2):
                off = 0.25 * which
                m = 12582912.0
                k1 = dve(lambda e, off=off: e.tensor_scalar(kk, ang, float(1 / (2 * np.pi)), off, ALU.mult, ALU.add), b, tok)
                k2 = dve(lambda e: e.tensor_scalar(kk, kk, m, m, ALU.add, ALU.subtract), k1)
                c1, c2 = 6.28125, 1.93500518798828125e-3
                c3 = 2 * np.pi - c1 - c2
                yield
                r1 = dve(lambda e: e.scalar_tensor_tensor(red, kk, -c1, ang, ALU.mult, ALU.add), k2, tok)
                r2 = dve(lambda e: e.scalar_tensor_tensor(red, kk, -c2, red, ALU.mult, ALU.add), r1)
                r3 = dve(lambda e: e.scalar_tensor_tensor(red, kk, -c3, red, ALU.mult, ALU.add), r2)
                lim = 3.1415925
                r4 = dve(lambda e, which=which: e.tensor_scalar(red, red, float(np.pi / 2) * which, lim, ALU.add, ALU.min), r3)
                r5 = dve(lambda e: e.tensor_scalar(red, red, -lim, None, ALU.max), r4)
                yield
                if which == 0:
                    tok = act(lambda e: e.activation(SN[:, :, 32:64], red, ACT.Sin), r5)
                    n1 = dve(lambda e: e.tensor_scalar(SN[:, :, 0:32], SN[:, :, 32:64], -1.0, None, ALU.mult), tok)
                else:
                    tok = act(lambda e: e.activation(CS[:, :, 0:32], red, ACT.Sin), r5)
                    n2 = dve(lambda e: e.tensor_copy(CS[:, :, 32:64], CS[:, :, 0:32]), tok)
                yield
            S["rope"] = [tok, n1, n2]

        ROPE_T = [ar(18688 + 64 * i, 64).rearrange("p (t n) -> p t n", t=2) for i in range(3)]

        row_tok, row_reads = {}, []

        def ev_small(st):
            while not (stage.avail() and banks.avail()):
                yield
            si, small, after = stage.get()
            sc = act(lambda e: e.activation(small[0:80, 0:256], gps[st.pair][0][0:80, 0:256], ACT.Copy), st.done, after)
            release(st, sc)
            yield
            j, bk, baft = banks.get()
            for t in range(2):
                tok = pe(lambda e, t=t, bk=bk: e.transpose(bk[:, 80 * t:80 * t + 80], small[0:80, t * P:(t + 1) * P],
                                                           ident[0:80, 0:80]), sc, baft, t_cst)
            stage.give(si, tok)
            while "r2w" not in S:
                yield
            c = [act(lambda e, t=t, bk=bk: e.activation(SM[:, t], bk[:, 80 * t:80 * t + 80], ACT.Copy,
                                                        scale=S["r2"][:, t:t + 1]), tok, S["r2w"]) for t in range(2)]
            banks.give(j, *c)
            S["sm"] = c
            side.append(k_rope())
            yield
            while not banks.avail():
                yield
            j, bk, baft = banks.get()
            for g in range(2):
                for t in range(2):
                    tok = pe(lambda e, g=g, t=t, bk=bk: e.matmul(bk[0:8, g * 256 + t * P:g * 256 + (t + 1) * P],
                                                          SM[:, t, 8 * g:8 * g + 8], ident, start=True, stop=True),
                             c, baft, t_cst)
            yield
            li, fp, ab, lf, F, u, M, en, one = ROWS
            gb = vec("gb", 0, 2, 8)
            w0 = S["r1_x"]
            o = dve(lambda e: e.memset(one, 1.0), S["r2_x"], dn_fg, mix_fg)
            a = dve(lambda e, bk=bk: e.tensor_scalar(li, bk[0:8, 0:256], gb[:, 0:1], None, ALU.add), tok, t_vec, S["r2_x"])
            b = dve(lambda e, bk=bk: e.tensor_scalar(fp, bk[0:8, 256:512], gb[:, 1:2], None, ALU.add), tok, t_vec, S["r2_x"])
            banks.give(j, a, b)
            yield
            c1 = act(lambda e: e.activation(ab, fp, ACT.Abs), b)
            c2 = act(lambda e: e.activation(ab, ab, ACT.Exp, scale=-1.0), c1)
            c3 = act(lambda e: e.activation(ab, ab, ACT.Ln, bias=1.0), c2)
            yield
            e1 = dve(lambda e: e.scalar_tensor_tensor(lf, fp, 0.0, ab, ALU.min, ALU.subtract), c3)
            e2 = dve(lambda e: e.tensor_tensor_scan(F, one, lf, 0.0, ALU.mult, ALU.add), e1, o)
            e3 = dve(lambda e: e.tensor_tensor(u, li, F, ALU.subtract), e2, a)
            e4 = dve(lambda e: e.tensor_tensor_scan(M, u, u, 0.0, ALU.max, ALU.max), e3)
            e5 = dve(lambda e: e.tensor_tensor(en, F, M, ALU.add), e4)
            yield
            x1 = act(lambda e: e.activation(en, en, ACT.Exp, scale=-1.0), e5)
            yield from pause(8)
            while not banks.avail():
                yield
            j, bk, baft = banks.get()
            uN, eN = stat(16), stat(16)
            for g, src in enumerate((u, en)):
                for t in range(2):
                    tok = pe(lambda e, g=g, t=t, src=src, bk=bk: e.matmul(bk[:, 16 * g + 8 * t:16 * g + 8 * t + 8],
                                                                   src[:, t * P:(t + 1) * P], CST[0:8, 0:8],
                                                                   start=True, stop=True), e3, x1, baft, t_cst)
            yield
            c1 = dve(lambda e, bk=bk: e.tensor_copy(uN, bk[:, 0:16]), tok)
            c2 = dve(lambda e, bk=bk: e.tensor_copy(eN, bk[:, 16:32]), tok)
            banks.give(j, c1, c2)
            row_tok.update(uN=uN, eN=eN, w=[c1, c2, e4])

        def k_rope():
            while "rope" not in S:
                yield
            kss = stat(2)
            kr = SM[:, :, 16:80]
            S["kss"], S["kssw"] = kss, sumsq(kr, S["sm"], kss)
            gk = vec("gkr", 0, 64)
            tmp = ar(18432, 256).rearrange("p (a t n) -> p a t n", a=2, t=2)
            tg, ts = tmp[:, 0], tmp[:, 1]
            g = [dve(lambda e, t=t: e.tensor_tensor(tg[:, t], kr[:, t], gk, ALU.mult), S["sm"], t_vec, S["r2_x"],
                     S["r2_reads"]) for t in range(2)]
            yield
            a = dve(lambda e: e.tensor_tensor(ts[:, :, 0:32], tg[:, :, 32:64], SN[:, :, 0:32], ALU.mult), g, S["rope"])
            b = dve(lambda e: e.tensor_tensor(ts[:, :, 32:64], tg[:, :, 0:32], SN[:, :, 32:64], ALU.mult), g, S["rope"])
            c = dve(lambda e: e.tensor_tensor(KROPE, tg, CS, ALU.mult), g, S["rope"])
            yield
            S["krope"] = dve(lambda e: e.tensor_tensor(KROPE, KROPE, ts, ALU.add), a, b, c)

        qk2_ready = [None] * 16
        pre_zero = []

        def ev_qk2(n):
            def f(st):
                while not stage.avail() or "r2w" not in S:
                    yield
                i, b, after = stage_get()
                c = copy_scaled(st, b, S["r2"], S["r2w"], after)
                release(st, *c)
                if n == 0:
                    for k in range(2):
                        pre_zero.append(dve(lambda e, k=k: e.memset(PRE.bufs[k][:, :, 0:3], 0.0), S["r2_x"]))
                yield
                for pair in range(2):
                    while not (banks.avail() and PRE.avail()):
                        yield
                    j, bk, baft = banks.get()
                    pi, pre, paft = PRE.get()
                    for k in range(2):
                        for t in range(2):
                            cc = (2 * pair + k) * P
                            tok = pe(lambda e, o=bk[:, k * 256 + t * P:k * 256 + (t + 1) * P], s=b[:, t, cc:cc + P]:
                                     e.transpose(o, s, ident), c, baft, t_cst)
                    yield
                    tk = act(lambda e, bk=bk, pre=pre: e.activation(
                        pre[:, :, 3:259], bk[:, :].rearrange("p (k n) -> p k n", k=2), ACT.Copy), tok, paft, S["r2_x"])
                    banks.give(j, tk)
                    yield
                    last = [None, None]
                    ct = 4 * n + 2 * pair
                    for m in range(4):
                        for k in range(2):
                            w = vec("conv_w", (ct + k) * 4 + m)
                            s, o = pre[:, k, m:m + 256], QK2[:, ct + k, :]
                            if m == 0:
                                last[k] = dve(lambda e, s=s, o=o, w=w: e.tensor_scalar(o, s, w, None, ALU.mult),
                                              tk, t_vec, pre_zero, S["r2_reads"], S["r2_x"])
                            else:
                                last[k] = dve(lambda e, s=s, o=o, w=w: e.scalar_tensor_tensor(
                                    o, s, w, o, ALU.mult, ALU.add), last[k])
                    yield
                    o2 = QK2[:, ct:ct + 2, :]
                    th = pre[:, :, 3:259]
                    tt = act(lambda e, o2=o2, th=th: e.activation(th, o2, ACT.Tanh, scale=0.5), last)
                    v = dve(lambda e, o2=o2, th=th: e.scalar_tensor_tensor(o2, th, 1.0, o2, ALU.add, ALU.mult), tt)
                    PRE.give(pi, v)
                    qk2_ready[ct] = qk2_ready[ct + 1] = v
                stage.give(i, tok)
            return f

        v2_ready = [None] * 4
        ml_read = []

        def ev_v2(n):
            def f(st):
                w = [S["r2_reads"], S["r2_x"]]
                if n == 0:
                    S["v2one"] = dve(lambda e: e.memset(V2[:, :, :, 256:258], 1.0), w)
                c = [act(lambda e, t=t: e.activation(
                    V2[:, t, 2 * n:2 * n + 2, 0:256], gps[st.pair][t][:, :].rearrange("p (h n) -> p h n", h=2),
                    ACT.Copy, scale=S["r2"][:, t:t + 1]), st.done, S["r2w"], w) for t in range(2)]
                release(st, *c)
                v2_ready[n] = c
                return
                yield
            return f

        oz = {}

        def ev_o(n):
            def f(st):
                while not stage.avail():
                    yield
                i, b, after = stage_get()
                t = tanh_scaled(st, b, S["r2h"], S["r2hw"], after)
                release(st, *t)
                oz["o", n] = (i, b, t)
            return f

        def silu_of(st, done):
            while not stage.avail(2):
                yield
            i, b, after = stage_get()
            i2, b2, after2 = stage_get()
            t = tanh_scaled(st, b, S["r2h"], S["r2hw"], after)
            z = copy_scaled(st, b2, S["r2h"], S["r2hw"], after2)
            release(st, *t, *z)
            s = dve(lambda e: e.scalar_tensor_tensor(b, b, 1.0, b2, ALU.add, ALU.mult), t, z)
            stage.give(i2, s)
            done(i, b, s)

        def ev_z(n):
            def f(st):
                def done(i, b, s):
                    oi, ob, ot = oz["o", n]
                    m = dve(lambda e: e.scalar_tensor_tensor(b, ob, 1.0, b, ALU.add, ALU.mult), s, ot)
                    stage.give(oi, m)
                    oz["oz", n] = (i, b, m)
                yield from silu_of(st, done)
                side.append(ml_pair(n))
            return f

        def ml_pair(n):
            i, b, m = oz["oz", n]
            outs, left = [], [2]
            for h in (2 * n, 2 * n + 1):
                while not (ML_E.avail() and ML_S.avail()):
                    yield
                spawn(ml_head(h, b, m, outs, left))
                for _ in range(3):
                    yield
            while left[0]:
                yield
            yield from pause(3)
            yield from turn(b, outs, TB, 4 * n, ("mlstm_g", 4 * n), free=lambda r: stage.give(i, *r))

        def ml_head(h, ob, om, outs, left):
            ei, E, eaft = ML_E.get()
            si, ST, saft = ML_S.get()
            while not banks.avail(2):
                yield
            j1, f1, a1 = banks.get()
            j2, f2, a2 = banks.get()
            q, k = QK2[:, h, :], QK2[:, 8 + h, :]
            w = [qk2_ready[h], qk2_ready[8 + h], row_tok["w"], S["r2_x"]]
            pe(lambda e: e.matmul(f2[:, 0:256], CST[0:8, h:h + 1].to_broadcast([8, P]), ROWS[6], start=True, stop=True),
               w, a2, t_cst)
            pe(lambda e: e.matmul(f1[:, 0:256], k[:, 0:P], q, start=True, stop=True), w, a1)
            tok = pe(lambda e: e.matmul(f1[:, 256:384], k[:, P:256], q[:, P:256], start=True, stop=True))
            ml_read.append(tok)
            yield
            uN, eN = row_tok["uN"], row_tok["eN"]
            E3 = E.rearrange("p (c n) -> p c n", c=3)
            row_reads.append(tok)
            mk = CST[:, C_MASKT:C_MASKT + P].unsqueeze(1).to_broadcast([P, 2, P])
            a = dve(lambda e: e.tensor_tensor(E3[:, 0:3:2, :], mk, f2[:, 0:256].rearrange("p (c n) -> p c n", c=2),
                                              ALU.subtract), tok, eaft, S["r2_x"])
            x = [act(lambda e: e.activation(E3[:, 1], f2[:, P:256], ACT.Exp, bias=uN[:, h:h + 1], scale=-1.0), a,
                     row_tok["w"], eaft, S["r2_x"]),
                 act(lambda e: e.activation(E3[:, 0], E3[:, 0], ACT.Exp, bias=uN[:, h:h + 1]), a, row_tok["w"]),
                 act(lambda e: e.activation(E3[:, 2], E3[:, 2], ACT.Exp, bias=uN[:, 8 + h:9 + h]), a, row_tok["w"])]
            banks.give(j2, *x, a)
            s = dve(lambda e: e.scalar_tensor_tensor(ST, f1[:, 0:384], float(P ** -0.5) * 0.25, E, ALU.mult, ALU.mult),
                    x, saft)
            banks.give(j1, s)
            ML_E.give(ei, s)
            yield
            yield
            yield
            while not banks.avail(2):
                yield
            j1, b1, a1 = banks.get()
            j2, b2, a2 = banks.get()
            vv = v2_ready[h // 2]
            pe(lambda e: e.matmul(b1[:, 0:258], ST[:, 0:P], V2[:, 0, h, :], start=True, stop=True), s, a1, vv, S["v2one"])
            pe(lambda e: e.matmul(b2[:, 0:258], ST[:, P:256], V2[:, 0, h, :], start=True, stop=False), a2)
            tok = pe(lambda e: e.matmul(b2[:, 0:258], ST[:, 256:384], V2[:, 1, h, :], start=False, stop=True))
            ML_S.give(si, tok)
            ml_read.append(tok)
            yield
            dn, ssn, t1, t2, sc = stat(2), stat(2), stat(2), stat(2), stat(2)
            bb = (b1, b2)
            q1 = []
            for t in range(2):
                q1.append(act(lambda e, t=t: e.activation(junk[:, 0:256], bb[t][:, 0:256], ACT.Square,
                                                          accum_out=ssn[:, t:t + 1]), tok, junk_tok[0]))
                junk_tok[0] = q1[-1]
            d0 = [dve(lambda e, t=t: e.tensor_scalar(t1[:, t:t + 1], bb[t][:, 256:257], -1.0,
                                                     eN[:, 8 * t + h:8 * t + h + 1], ALU.mult, ALU.max),
                      q1[t], row_tok["w"]) for t in range(2)]
            d1 = [dve(lambda e, t=t: e.tensor_tensor(dn[:, t:t + 1], bb[t][:, 256:257], t1[:, t:t + 1], ALU.max), d0[t])
                  for t in range(2)]
            d2 = dve(lambda e: e.reciprocal(dn, dn), d1)
            d3 = dve(lambda e: e.tensor_tensor(t1, dn, dn, ALU.mult), d2)
            yield
            d4 = dve(lambda e: e.tensor_tensor(t1, t1, ssn, ALU.mult), d3, q1)
            d5 = dve(lambda e: e.tensor_scalar(t1, t1, 1.0 / 256, 1e-6, ALU.mult, ALU.add), d4)
            pw = alone(lambda e: e.tensor_tensor(t2, t1, half[:, 0:2], ALU.pow), d5, t_half)
            d6 = dve(lambda e: e.scalar_tensor_tensor(sc, dn, 0.5, t2, ALU.mult, ALU.mult), pw)
            yield
            c0 = (h % 2) * 256
            o = [dve(lambda e, t=t: e.scalar_tensor_tensor(ob[:, t, c0:c0 + 256], bb[t][:, 0:256], sc[:, t:t + 1],
                                                           ob[:, t, c0:c0 + 256], ALU.mult, ALU.mult), d6, om, q1)
                 for t in range(2)]
            banks.give(j1, o[0], d1[0])
            banks.give(j2, o[1], d1[1])
            outs.extend(o)
            left[0] -= 1

        ga, spilled = {}, {}

        def ev_ga(n):
            def f(st):
                while not stage.avail():
                    yield
                i, b, after = stage_get()
                t = tanh_scaled(st, b, S["r2h"], S["r2hw"], after)
                release(st, *t)
                ga[n] = (i, b, t)
            return f

        def flat(b):
            return b.rearrange("p t n -> p (t n)")

        def ev_ya(n):
            def f(st):
                i, b, t = ga[n]
                y = [dve(lambda e, t=t: e.scalar_tensor_tensor(b[:, t], b[:, t], 1.0, gps[st.pair][t][:, :], ALU.add,
                                                               ALU.mult), st.done, ga[n][2]) for t in range(2)]
                release(st, *y)
                s = once(f"d_ys{n}", sp, d["ys"][n].rearrange("p (t n) -> p t n", t=2), b, y)
                spilled["y", n] = s
                stage.give(i, s)
                return
                yield
            return f

        HQT = ar(4096, 2048).rearrange("p (c n) -> p c n", c=8)
        HKT = ar(6144, 2048).rearrange("p (c n) -> p c n", c=8)
        HQR = ar(8192, 1024).rearrange("p (c n) -> p c n", c=4)
        HKR = ar(9216, 2048).rearrange("p (c a n) -> p c a n", c=4, a=2)
        HV = ar(11264, 2048).rearrange("p (t n) -> p t n", t=2)
        ZB = [ar(13312 + 1024 * i, 1024).rearrange("p (t n) -> p t n", t=2) for i in range(3)]
        at_p = Slots([ar(16384 + 384 * i, 384) for i in range(3)])
        at_pt = Slots([ar(17536 + 384 * i, 384) for i in range(3)])

        def ev_lat(which):
            def f(st):
                if which == 0:
                    t_kz.extend(dve(lambda e, a=a: e.memset(HKR[64 - 64 * a:128 - 64 * a, :, a, :], 0.0), ml_read,
                                    row_tok["w"], row_reads) for a in range(2))
                while not stage.avail():
                    yield
                i, b, after = stage_get()
                c = copy_scaled(st, b, S["r2"], S["r2w"], after)
                release(st, *c)
                ss = stat(2)
                q = sumsq(b, c, ss)
                S["lat", which] = rsqrt_of(ss, 2, 1e-6, 1.0 / 512, 2, q)
                yield
                yield from turn(b, c, TB, 8 + 4 * which, ("q_lat_g" if which == 0 else "kv_lat_g", 0),
                                free=lambda r: stage.give(i, *r, *q))
            return f

        zb_tok, zb_read = {}, {}

        def ev_zb(n):
            def f(st):
                def done(i, b, s):
                    c = dve(lambda e: e.tensor_copy(ZB[n % 3], b), s, ml_read, zb_read.get(n - 3))
                    stage.give(i, c)
                    zb_tok[n] = c
                yield from silu_of(st, done)
            return f

        def ev_gb(n):
            def f(st):
                while not stage.avail():
                    yield
                i, b, after = stage_get()
                t = tanh_scaled(st, b, S["r2h"], S["r2hw"], after)
                release(st, *t)
                s = once(f"d_gs{n}", sp, d["gs"][n].rearrange("p (t n) -> p t n", t=2), b, t)
                spilled["g", n] = s
                stage.give(i, s)
            return f

        H = {0: dict(nq=0, nk=0, nv=0, qt={}, kt={}, qr=None, kr=None, v={}), 1: dict(nq=0, nk=0, nv=0, qt={}, kt={}, qr=None, kr=None, v={})}
        at_read = []
        ssq = {}
        for hf in range(2):
            H[hf].update(ssq=stat(16).rearrange("p (t h) -> p t h", t=2), ssr=stat(16).rearrange("p (t h) -> p t h", t=2),
                         ssk=stat(16).rearrange("p (t h) -> p t h", t=2), ssqw=[], ssrw=None, rk=[None, None])

        def head_sq(b, c, nh, dst):
            j, sq, after = stage.get()
            s4 = sq.rearrange("p (t n) -> p t n", t=2)
            a = dve(lambda e: e.tensor_tensor(s4, b, b, ALU.mult), c, after)
            r = [dve(lambda e, t=t: e.tensor_reduce(dst[:, t], s4[:, t].rearrange("p (h n) -> p h n", h=nh), AX.X,
                                                    ALU.add), a) for t in range(2)]
            stage.give(j, *r)
            return r

        def to_channels(b, w, dst, c0, scale, war):
            toks = []
            for pair in range(2):
                while not banks.avail():
                    yield
                j, bk, baft = banks.get()
                for k in range(2):
                    for t in range(2):
                        cc = (2 * pair + k) * P
                        tok = pe(lambda e, o=bk[:, k * 256 + t * P:k * 256 + (t + 1) * P], s=b[:, t, cc:cc + P]:
                                 e.transpose(o, s, ident), w, baft, t_cst)
                yield
                o = dst[:, c0 + 2 * pair:c0 + 2 * pair + 2, :]
                s = bk[:, :].rearrange("p (k n) -> p k n", k=2)
                if scale is None:
                    tk = act(lambda e, o=o, s=s: e.activation(o, s, ACT.Copy), tok, war)
                else:
                    tk = act(lambda e, o=o, s=s: e.activation(o, s, ACT.Copy, scale=scale[0]), tok, war, scale[1])
                banks.give(j, tk)
                toks.append(tk)
            return toks, tok

        def ev_uqn(hf, n):
            def f(st):
                while not stage.avail(2):
                    yield
                i, b, after = stage_get()
                c = copy_scaled(st, b, S["lat", 0][0], S["lat", 0][1], after)
                release(st, *c)
                H[hf]["ssqw"] += head_sq(b, c, 4, H[hf]["ssq"][:, :, 4 * n:4 * n + 4])
                yield from pause(2)
                toks, rd = yield from to_channels(b, c, HQT, 4 * n, (S["gqk"], S["gqkw"]), [ml_read, at_read])
                for k in range(4):
                    H[hf]["qt"][4 * n + k] = toks[k // 2]
                stage.give(i, rd, *H[hf]["ssqw"])
            return f

        def ev_uqr(hf):
            def f(st):
                while not stage.avail(3):
                    yield
                i, b, after = stage_get()
                c = copy_scaled(st, b, S["lat", 0][0], S["lat", 0][1], after)
                release(st, *c)
                H[hf]["ssrw"] = head_sq(b, c, 8, H[hf]["ssr"])
                i2, b2, after2 = stage_get()
                yield
                al = []
                for t in range(2):
                    v = b[:, t].rearrange("p (h n) -> p h n", h=8)
                    o = b2[:, t].rearrange("p (h n) -> p h n", h=8)
                    g = vec("gqr", 0, 64).unsqueeze(1).to_broadcast([P, 8, 64])

                    def bc(ap, n):
                        return ap.unsqueeze(1).to_broadcast([P, 8, n])

                    a = dve(lambda e, v=v, g=g: e.tensor_tensor(v, v, g, ALU.mult), c, H[hf]["ssrw"], t_vec)
                    m1 = dve(lambda e, t=t, v=v, o=o: e.tensor_tensor(o[:, :, 0:32], v[:, :, 32:64], bc(SN[:, t, 0:32], 32),
                                                                      ALU.mult), a, after2, S["rope"])
                    m2 = dve(lambda e, t=t, v=v, o=o: e.tensor_tensor(o[:, :, 32:64], v[:, :, 0:32], bc(SN[:, t, 32:64], 32),
                                                                      ALU.mult), a, after2, S["rope"])
                    m3 = dve(lambda e, t=t, v=v: e.tensor_tensor(v, v, bc(CS[:, t], 64), ALU.mult), a, m1, m2, S["rope"])
                    al.append(dve(lambda e, v=v, o=o: e.tensor_tensor(o, o, v, ALU.add), m1, m2, m3))
                stage.give(i, *al)
                yield from pause(8)
                toks, rd = yield from to_channels(b2, al, HQR, 0, None, [ml_read, at_read])
                stage.give(i2, rd)
                H[hf]["qr"] = toks
                while len(H[hf]["ssqw"]) < 4:
                    yield
                tot = stat(16)
                sa = dve(lambda e: e.tensor_tensor(tot.rearrange("p (t h) -> p t h", t=2), H[hf]["ssq"], H[hf]["ssr"], ALU.add),
                         H[hf]["ssqw"], H[hf]["ssrw"])
                r, rw = rsqrt_of(tot, 2, 1e-6, 1.0 / 192, 16, sa)
                w = dve(lambda e: e.tensor_scalar(r, r, float(192 ** -0.5), None, ALU.mult), rw)
                H[hf]["sc"], H[hf]["scw"] = r.rearrange("p (t h) -> p t h", t=2), w
            return f

        def ev_ukn(hf, n):
            def f(st):
                while not stage.avail(2):
                    yield
                i, b, after = stage_get()
                c = copy_scaled(st, b, S["lat", 1][0], S["lat", 1][1], after)
                release(st, *c)
                ssk = H[hf]["ssk"][:, :, 4 * n:4 * n + 4]
                q = head_sq(b, c, 4, ssk)
                tot = stat(8)
                t3 = tot.rearrange("p (t h) -> p t h", t=2)
                a = [dve(lambda e, t=t: e.tensor_scalar(t3[:, t], ssk[:, t], S["kss"][:, t:t + 1], None, ALU.add), q, S["kssw"])
                     for t in range(2)]
                r, rw = rsqrt_of(tot, 2, 1e-6, 1.0 / 192, 8, a)
                H[hf]["rk"][n] = (r.rearrange("p (t h) -> p t h", t=2), rw)
                yield from pause(3)
                v = b.rearrange("p t (h n) -> p (t h) n", h=4)
                m = dve(lambda e: e.tensor_tensor(v, v, r.unsqueeze(2).to_broadcast([P, 8, P]), ALU.mult), rw, c, q)
                yield from pause(3)
                toks, rd = yield from to_channels(b, m, HKT, 4 * n, None, [ml_read, at_read])
                for k in range(4):
                    H[hf]["kt"][4 * n + k] = toks[k // 2]
                stage.give(i, rd)
                if n == 1:
                    while H[hf]["rk"][0] is None or not stage.avail():
                        yield
                    i, b, after = stage_get()
                    al = []
                    for n2 in range(2):
                        rr, rrw = H[hf]["rk"][n2]
                        for t in range(2):
                            o = b[:, t, 256 * n2:256 * n2 + 256].rearrange("p (h n) -> p h n", h=4)
                            al.append(dve(lambda e, o=o, t=t, rr=rr: e.tensor_tensor(
                                o, KROPE[:, t].unsqueeze(1).to_broadcast([P, 4, 64]),
                                rr[:, t].unsqueeze(2).to_broadcast([P, 4, 64]), ALU.mult), rrw, after, S["krope"]))
                    yield from pause(4)
                    toks = []
                    for pair in range(2):
                        while not banks.avail():
                            yield
                        j, bk, baft = banks.get()
                        for k in range(2):
                            for t in range(2):
                                cc = (2 * pair + k) * P
                                tok = pe(lambda e, o=bk[:, k * 256 + t * P:k * 256 + (t + 1) * P], s=b[:, t, cc:cc + P]:
                                         e.transpose(o, s, ident), al, baft, t_cst)
                        yield
                        s3 = bk[:, :].rearrange("p (k n) -> p k n", k=2)
                        ev = [act(lambda e, a=a, s3=s3, pair=pair: e.activation(
                            HKR[64 * a:64 * a + 64, 2 * pair:2 * pair + 2, a, :], s3[64 * a:64 * a + 64], ACT.Copy),
                            tok, ml_read, at_read) for a in range(2)]
                        banks.give(j, *ev)
                        toks += ev
                    stage.give(i, tok)
                    H[hf]["kr"] = toks
            return f

        def ev_uv(hf, n):
            def f(st):
                c = copy_scaled(st, HV[:, :, 512 * n:512 * n + 512], S["lat", 1][0], S["lat", 1][1], [ml_read, at_read])
                release(st, *c)
                H[hf]["v"][n] = c
                if n == 1:
                    side.append(at_heads(hf))
                return
                yield
            return f

        def at_quad(n, i, b, outs, left):
            while left[0]:
                yield
            zb_read[n] = list(outs)
            yield from pause(2)
            yield from turn(b, outs, TB, 4 * n, free=lambda r: stage.give(i, *r))

        t_kz = []
        AT_PAUSE = (3, 3)
        AT_SPACE = 2

        def at_heads(hf):
            mine = []
            H[hf]["left"] = 8
            while H[hf]["kr"] is None or "sc" not in H[hf]:
                yield
            for qd in range(2):
                n = 2 * hf + qd
                while n not in zb_tok or not stage.avail():
                    yield
                i, b, after = stage_get()
                outs, left = [], [4]
                for hh in range(4):
                    while not (at_p.avail() and at_pt.avail()):
                        yield
                    spawn(at_head(hf, 4 * qd + hh, ZB[n % 3], zb_tok[n], b, after, outs, left, mine))
                    yield from pause(AT_SPACE)
                side.append(at_quad(n, i, b, outs, left))
            while H[hf]["left"]:
                yield
            at_read.extend(mine)
            S["att", hf] = True

        def at_head(hf, h, zb, zw, ob, oaft, outs, left, mine):
            hd = H[hf]
            pi, pb, paft = at_p.get()
            ti, tb, taft = at_pt.get()
            while not banks.avail():
                yield
            j, bk, kaft = banks.get()
            ct = h // 2
            w = [hd["qt"][h], hd["kt"][h], hd["qr"], hd["kr"], t_kz, kaft]
            for it, (c0, n) in enumerate(((0, 128), (128, 256))):
                pe(lambda e, it=it, c0=c0, n=n: e.matmul(bk[:, c0:c0 + n], HQT[:, h, it * P:(it + 1) * P],
                                                         HKT[:, h, 0:n], start=True, stop=False), w)
                tok = pe(lambda e, it=it, c0=c0, n=n: e.matmul(bk[:, c0:c0 + n], HQR[:, ct, it * P:(it + 1) * P],
                                                               HKR[:, ct, h % 2, 0:n], start=False, stop=True))
            mine.append(tok)
            yield from pause(AT_PAUSE[0])
            mx, nb, sm, rc = stat(2), stat(2), stat(2), stat(2)
            s = dve(lambda e: e.tensor_tensor(pb, bk[:, 0:384], CST[:, C_MASK:C_MASK + 384], ALU.add), tok, paft, t_cst, ml_read)
            banks.give(j, s)
            m = [dve(lambda e: e.tensor_reduce(mx[:, 0:1], pb[:, 0:128], AX.X, ALU.max), s),
                 dve(lambda e: e.tensor_reduce(mx[:, 1:2], pb[:, 128:384], AX.X, ALU.max), s)]
            sc = hd["sc"][:, :, h]
            b = dve(lambda e: e.scalar_tensor_tensor(nb, mx, -1.0, sc, ALU.mult, ALU.mult), m, hd["scw"])
            ex = [act(lambda e, t=t, a=a, z=z: e.activation(pb[:, a:z], pb[:, a:z], ACT.Exp, bias=nb[:, t:t + 1],
                                                            scale=hd["sc"][:, t, h:h + 1], accum_out=sm[:, t:t + 1]), b)
                  for t, (a, z) in enumerate(((0, 128), (128, 384)))]
            yield from pause(AT_PAUSE[1])
            rr = dve(lambda e: e.reciprocal(rc, sm), ex)
            while not banks.avail():
                yield
            j, bk2, kaft = banks.get()
            for c in range(3):
                tok = pe(lambda e, c=c: e.transpose(bk2[:, c * P:(c + 1) * P], pb[:, c * P:(c + 1) * P], ident),
                         ex, kaft, t_cst)
            at_p.give(pi, tok)
            yield
            cp = act(lambda e: e.activation(tb, bk2[:, 0:384], ACT.Copy), tok, taft, ml_read)
            banks.give(j, cp)
            yield
            while not banks.avail():
                yield
            j, bk3, kaft = banks.get()
            vw = hd["v"][h // 4]
            v = HV[:, :, h * P:(h + 1) * P]
            pe(lambda e: e.matmul(bk3[:, 0:P], tb[:, 0:P], v[:, 0], start=True, stop=True), cp, vw, kaft)
            pe(lambda e: e.matmul(bk3[:, P:256], tb[:, P:256], v[:, 0], start=True, stop=False))
            tok = pe(lambda e: e.matmul(bk3[:, P:256], tb[:, 256:384], v[:, 1], start=False, stop=True))
            at_pt.give(ti, tok)
            mine.append(tok)
            yield
            o = [dve(lambda e, t=t: e.scalar_tensor_tensor(
                ob[:, t, (h % 4) * P:(h % 4 + 1) * P], bk3[:, t * P:(t + 1) * P], rc[:, t:t + 1],
                zb[:, t, (h % 4) * P:(h % 4 + 1) * P], ALU.mult, ALU.mult), tok, rr, oaft, zw) for t in range(2)]
            banks.give(j, *o)
            outs.extend(o)
            mine.extend(o)
            left[0] -= 1
            hd["left"] -= 1

        ld_sem = [sem(f"d_ld{i}") for i in range(4)]
        loaded = {}

        def reload(*what):
            for name, n in what:
                while not stage.avail():
                    yield
                i, b, after = stage.get()
                src = d[{"y": "ys", "g": "gs", "x": "x2s"}[name]][n]
                w = spilled[name, n] if name != "x" else S["r2_reads"]
                loaded[name, n] = (i, nat(b), dma(sp, b, src, ld_sem[i], w, after))

        def ev_yb(n, part):
            def f(st):
                while ("g", n) not in loaded or ("y", n) not in loaded:
                    yield
                gi, g, gt = loaded.pop(("g", n))
                yi, y, yt = loaded.pop(("y", n))
                m = [dve(lambda e, t=t: e.scalar_tensor_tensor(g[:, t], g[:, t], 1.0, gps[st.pair][t][:, :], ALU.add,
                                                               ALU.mult), st.done, gt) for t in range(2)]
                release(st, *m)
                s = dve(lambda e: e.tensor_tensor(y, y, g, ALU.add), m, yt)
                stage.give(gi, s)
                if part == 0:
                    spilled["y", n] = once(f"d_yt{n}", sp, d["ys"][n].rearrange("p (t n) -> p t n", t=2), y, s)
                    stage.give(yi, spilled["y", n])
                    return
                yield from pause(3)
                if n == 0:
                    clear(TA)
                yield from turn(y, s, TA, 4 * n, scale=0.5, free=lambda r: stage.give(yi, *r))
            return f

        out_sem = [sem(f"d_out{i}") for i in range(4)]
        out_toks = []
        od = out.rearrange("(t p) n -> p t n", p=P)

        def ev_out(n):
            def f(st):
                while ("x", n) not in loaded:
                    yield
                xi, x, xt = loaded.pop(("x", n))
                o = [dve(lambda e, t=t: e.tensor_tensor(x[:, t], x[:, t], gps[st.pair][t][:, :], ALU.add), st.done, xt)
                     for t in range(2)]
                release(st, *o)
                s = dma(sp, od[:, :, n * 512:(n + 1) * 512], x, out_sem[n], o)
                out_toks.append(s)
                stage.give(xi, s)
            return f

        for n in range(2):
            Stripe(f"gate{n}", "w_in", 2 + n, 16, TA, 0, ev_gate(n))
            Stripe(f"a{n}", "w_in", n, 16, TA, 0, ev_a(n))
        for n in range(2):
            Stripe(f"q{n}", "w_in", 4 + n, 16, TA, 0, ev_qk(QT1, "q", n))
            Stripe(f"k{n}", "w_in", 6 + n, 16, TA, 0, ev_qk(KT1, "k", n))
            Stripe(f"v{n}", "w_in", 8 + n, 16, TA, 0, ev_v(n))
        for n in range(4):
            Stripe(f"mixc{n}", "w_out", n, 8, TB, 0, ev_mix0(n))
        for n in range(4):
            Stripe(f"mixa{n}", "w_out", n, 8, TB, 8, ev_mix1(n), kfirst=4)

        def up(c):
            for n in range(2):
                Stripe(f"up{c}{n}", "w_up", 2 * c + n, 16, TA, 0, ev_up(c, n))

        def down(c):
            for n in range(4):
                Stripe(f"down{c}{n}", "w_down", n, 8, TB, 8 * (c % 2), ev_down(c, n), kfirst=4 * c)

        up(0)
        for c in range(1, 8):
            up(c)
            down(c - 1)
        down(7)
        for n in range(4):
            Stripe(f"qk2{n}", "w_in_2", n, 16, TA, 0, ev_qk2(n))
            if n == 0:
                Stripe("small", "w_small", 0, 16, TA, 0, ev_small, cols=80, per=8)
        for n in range(4):
            Stripe(f"va{n}", "w_in_2", 4 + n, 16, TA, 0, ev_v2(n))
        for n in range(4):
            Stripe(f"oa{n}", "w_in_2", 8 + n, 16, TA, 0, ev_o(n))
            Stripe(f"za{n}", "w_in_2", 12 + n, 16, TA, 0, ev_z(n))
        for n in range(4):
            Stripe(f"ga{n}", "w_in_2", 22 + n, 16, TA, 0, ev_ga(n))
            Stripe(f"ya{n}", "w_a_2", n, 16, TB, 0, ev_ya(n))
        Stripe("cq", "w_in_2", 16, 16, TA, 0, ev_lat(0))
        Stripe("ckv", "w_in_2", 17, 16, TA, 0, ev_lat(1))

        def zb(n):
            Stripe(f"zb{n}", "w_in_2", 18 + n, 16, TA, 0, ev_zb(n))

        def gb(n):
            Stripe(f"gb{n}", "w_in_2", 26 + n, 16, TA, 0, ev_gb(n))

        def uq(hf):
            Stripe(f"uqr{hf}", "w_uq_2", 4 + hf, 4, TB, 8, ev_uqr(hf))
            for n in range(2):
                Stripe(f"uqn{hf}{n}", "w_uq_2", 2 * hf + n, 4, TB, 8, ev_uqn(hf, n))

        def uk(hf):
            for n in range(2):
                Stripe(f"ukn{hf}{n}", "w_ukv_2", 2 * hf + n, 4, TB, 12, ev_ukn(hf, n))

        def uv(hf):
            for n in range(2):
                Stripe(f"uv{hf}{n}", "w_ukv_2", 4 + 2 * hf + n, 4, TB, 12, ev_uv(hf, n))

        zb(0)
        uq(0)
        zb(1)
        uk(0)
        zb(2)
        uv(0)
        gb(0)
        zb(3)
        gb(1)
        uq(1)
        gb(2)
        uk(1)
        gb(3)
        uv(1)
        for n in range(4):
            Stripe(f"yb0{n}", "w_b_2", n, 8, TB, 0, ev_yb(n, 0))
        for n in range(4):
            Stripe(f"yb1{n}", "w_b_2", n, 8, TB, 8, ev_yb(n, 1), kfirst=4)
        for n in range(4):
            Stripe(f"out{n}", "w_out_2", n, 16, TA, 0, ev_out(n))

        def before(st):
            if st.name.startswith("up") and st.name[3] == "0":
                c = int(st.name[2])
                clear(TB, 8 * (c % 2), 8 * (c % 2) + 8)
            if st.name == "oa0":
                clear(TB)
            if st.name == "cq":
                clear(TB, 8, 16)
            if st.name == "uqr0":
                clear(TB, 0, 8)
            if st.name == "uqr1":
                until(lambda: ("att", 0) in S, "first half")
            if st.name == "yb00":
                clear(TB, 8, 16)
            if st.name[0:2] == "yb":
                side.append(reload(("g", int(st.name[3])), ("y", int(st.name[3]))))
            if st.name[0:3] == "out":
                side.append(reload(("x", int(st.name[3]))))

        S["gqk"] = stat(1)
        S["gqkw"] = dve(lambda e: e.tensor_tensor(S["gqk"], vec("gqn"), vec("gkn"), ALU.mult), t_vec)
        load_x()
        issue_dma(0)
        issue_dma(1)
        load_x()
        issue_dma(2)
        load_x()
        issue_dma(3)
        load_x()
        spawn(start1())
        split = 0
        for u in range(len(units)):
            while split <= min(u + AHEAD, 2 * u):
                issue_split(split)
                issue_dma(split + RAW)
                split += 1
            if units[u]["first"]:
                before(units[u]["st"])
            issue_mm(u)
            advance()
        drain()
        sp(lambda e: e.nop(), out_toks)

        for q in (pe, act, dve, pool, sp):
            q.count()
        block = ctx.enter_context(nc.Block())

        @block.sync
        def _(eng):
            sp.write(eng)

        @block.scalar
        def _(eng):
            act.write(eng)

        @block.vector
        def _(eng):
            dve.write(eng)

        @block.gpsimd
        def _(eng):
            pool.write(eng)

        @block.tensor
        def _(eng):
            pe.write(eng)


def _tiles(w):
    k, n = w.shape
    return w.reshape(k // 256, 2, 128, n // 512, 512).transpose(3, 0, 2, 1, 4).reshape(n // 512, k // 256, 128, 1024)


def _cols(v):
    return v.reshape(-1, 128).T


def kernel(**inputs):
    import concourse.bacc as _bacc
    from concourse import mybir as _mybir
    from concourse.bass_utils import run_bass_kernel_spmd as _run

    g = {k: np.asarray(v) for k, v in inputs.items()}
    A = {}
    A["x"] = g["x"][0]
    A["w_in"] = _tiles(g["w_in"][0])
    A["w_out"] = _tiles(g["w_out"][0])
    A["w_up"] = _tiles(g["w_up"][0])
    A["w_down"] = _tiles(g["w_down"][0])
    w2 = g["w_in_2"][0]
    o = dict(q=0, k=1024, v=2048, o=4096, i=6144, f=6152, z=6160, cq=8208, ckv=8720, kr=9232, zb=9296, ga=11344, gb=13392)
    big = np.concatenate([w2[:, 0:6144], w2[:, o["z"]:o["z"] + 2048], w2[:, o["cq"]:o["cq"] + 1024],
                          w2[:, o["zb"]:o["zb"] + 6144]], axis=1)
    A["w_in_2"] = _tiles(big)
    small = np.concatenate([w2[:, o["i"]:o["i"] + 16], w2[:, o["kr"]:o["kr"] + 64]], axis=1)
    A["w_small"] = small.reshape(2, 8, 128, 80).transpose(0, 2, 1, 3).reshape(2, 128, 640)
    A["w_a_2"] = _tiles(g["w_a_2"][0])
    uq = g["w_uq_2"][0].reshape(512, 16, 192)
    A["w_uq_2"] = _tiles(np.concatenate([uq[:, :, :128].reshape(512, 2048), uq[:, :, 128:].reshape(512, 1024)], axis=1))
    ukv = g["w_ukv_2"][0].reshape(512, 16, 256)
    A["w_ukv_2"] = _tiles(np.concatenate([ukv[:, :, :128].reshape(512, 2048), ukv[:, :, 128:].reshape(512, 2048)], axis=1))
    A["w_b_2"] = _tiles(g["w_b_2"][0])
    A["w_out_2"] = _tiles(g["w_out_2"][0])

    rows, kr = 4, 4
    r, c = np.arange(rows), np.arange(64)
    ridx = np.clip(r - kr // 2, 0, rows - kr)[:, None] + np.arange(kr)[None, :]
    cstart = np.clip(c - 8, 0, 48)
    cmask = (c[None, :] >= cstart[:, None]) & (c[None, :] < cstart[:, None] + 16)
    dr = ridx - r[:, None] + 7
    dc = np.clip(c[None, :] - c[:, None], -15, 15) + 15
    b = g["rpb"][0][:, dr[:, None, :, None], dc[None, :, None, :]]
    b = np.where(cmask[None, None, :, None, :], b, np.float32(NEG)).astype(np.float32)
    A["bias"] = b.reshape(8, 2, 2, 128, 256).transpose(0, 2, 3, 1, 4).reshape(8, 2, 128, 512)

    vecs = np.zeros((128, NVEC), np.float32)

    def put(name, v):
        vecs[0:v.shape[0], VEC[name][0]:VEC[name][0] + v.shape[1]] = v

    put("pre_mix_g", _cols(g["pre_mix_g"][0]))
    put("pre_mlp_g", _cols(g["pre_mlp_g"][0]))
    put("norm_g_2", _cols(g["norm_g_2"][0]))
    put("mlstm_g", _cols(g["mlstm_norm_g_2"][0]))
    put("ln_g", _cols(g["conv_ln_g"][0]))
    put("ln_b", _cols(g["conv_ln_b"][0]))
    put("b_dw", _cols(g["b_dw"][0]))
    put("w_dw", g["w_dw"][0].reshape(31, 8, 128).transpose(2, 1, 0).reshape(128, 248))
    put("conv_w", g["conv_w_2"][0].reshape(4, 16, 128).transpose(2, 1, 0).reshape(128, 64))
    put("q_lat_g", _cols(g["q_lat_g_2"][0]))
    put("kv_lat_g", _cols(g["kv_lat_g_2"][0]))
    put("gqn", g["q_norm_g_2"][0][:128, None])
    put("gkn", g["k_norm_g_2"][0][:128, None])
    put("gqr", np.broadcast_to(g["q_norm_g_2"][0][None, 128:], (128, 64)))
    put("gkr", np.broadcast_to(g["k_norm_g_2"][0][None, 128:], (128, 64)))
    put("gb", g["gate_bias_2"][0].reshape(2, 8).T)
    A["vec"] = vecs
    A["post_mix_g"] = np.broadcast_to(g["post_mix_g"][0][None, :], (128, 2048))
    A["post_mlp_g"] = np.broadcast_to(g["post_mlp_g"][0][None, :], (128, 2048))
    A["pos"] = g["positions_2"][0].astype(np.int32).reshape(2, 128).T

    cst = np.zeros((128, NCST), np.float32)
    cst[:, C_ID:C_ID + 128] = np.eye(128, dtype=np.float32)
    lower = np.where(np.arange(128)[None, :] <= np.arange(128)[:, None], 0.0, NEG).astype(np.float32)
    cst[:, C_MASK:C_MASK + 128] = lower
    cst[:, C_MASK + 256:C_MASK + 384] = lower
    cst[:, C_MASKT:C_MASKT + 128] = lower.T
    cst[:, C_INVF:C_INVF + 32] = np.exp(np.float32(-np.log(10000.0)) * np.arange(0, 64, 2, dtype=np.float32)
                                       / np.float32(64))[None, :]
    A["cst"] = cst

    nc = _bacc.Bacc("TRN2", target_bir_lowering=False, num_devices=1)
    arrays, aps = {}, {}
    for name, a in A.items():
        a = np.ascontiguousarray(a)
        arrays[f"in_{name}"] = a
        aps[name] = nc.dram_tensor(f"in_{name}", a.shape, _mybir.dt.from_np(a.dtype), kind="ExternalInput").ap()
    for name in ("x2s", "ys", "gs"):
        aps[name] = nc.dram_tensor(f"keep_{name}", (4, 128, 1024), F32).ap()
    out = nc.dram_tensor("out_0", (256, 2048), F32, kind="ExternalOutput").ap()
    bass_two_blocks(nc, aps, out)
    res = _run(nc, [arrays], core_ids=[0])
    return np.asarray(res.results[0]["out_0"]).reshape(1, 256, 2048)
```
